# Optimizing a Trainium2 kernel written in Bass

```python
import math
import jax, jax.numpy as jnp
from jax import lax
import numpy as np

D_MODEL = 1024
BATCH = 1
SEQ = 1024
DEPTH = 2
DEC_BATCH = 8
DEC_SEQ = 8
PAST_LEN = 1024
PAGE_SIZE = 128

N_A = (DEPTH + 1) // 2
N_C = DEPTH // 2
HD = 64
H_A = (D_MODEL // 2) // HD
KVH = 2
HPG = H_A // KVH
L_CMP = 32
L_SEL = 64
N_SEL = 8
WINDOW = 512
ROPE_THETA = 10000.0
Q_BLOCK = 128
FORCE_BONUS = 1.0e4
NEG_INF = -1.0e30
TINY = 1.0e-30
C_B = D_MODEL // 2
CONV_W = 31
D_C = D_MODEL
POOL_WINDOWS = (2, 4, 8, 16)
N_POOL_GROUPS = 4
G_C = D_C // N_POOL_GROUPS
POOL_HIST = max(POOL_WINDOWS) - 1
D_FF = int(math.ceil(8 * D_MODEL / 3 / 256)) * 256
ALPHA = (2 * DEPTH) ** 0.25
BETA = (8 * DEPTH) ** -0.25
Q_COLS = H_A * HD
KV_COLS = KVH * HD
GATE_COLS = 3 * H_A
IN_A = Q_COLS + 6 * KV_COLS + GATE_COLS + 2 * C_B
OUT_A = Q_COLS + C_B

kernel_name = 'nsa_conformer_pool_deepnorm_step'

def _layer_norm(x, g, b, eps=1e-5):
    xf = x.astype(jnp.float32)
    mu = jnp.mean(xf, -1, keepdims=True)
    var = jnp.mean(jnp.square(xf - mu), -1, keepdims=True)
    return ((xf - mu) * lax.rsqrt(var + eps) * g + b).astype(x.dtype)

def _rope(x, pos):
    half = HD // 2
    inv = ROPE_THETA ** (-jnp.arange(half, dtype=jnp.float32) / half)
    ang = pos.astype(jnp.float32)[:, None] * inv[None, :]
    cos = jnp.cos(ang)[None, :, None, :]
    sin = jnp.sin(ang)[None, :, None, :]
    xf = x.astype(jnp.float32)
    x1, x2 = xf[..., :half], xf[..., half:]
    return jnp.concatenate([x1 * cos - x2 * sin, x2 * cos + x1 * sin], -1).astype(x.dtype)

def _masked_softmax(s, mask, axes):
    s = jnp.where(mask, s.astype(jnp.float32), NEG_INF)
    m = jnp.max(s, axis=axes, keepdims=True)
    e = jnp.where(mask, jnp.exp(s - m), 0.0)
    return e / jnp.maximum(jnp.sum(e, axis=axes, keepdims=True), TINY)

def _last_rows(a, n):
    if a.shape[1] >= n:
        return a[:, a.shape[1] - n:]
    pad = [(0, 0)] * a.ndim
    pad[1] = (n - a.shape[1], 0)
    return jnp.pad(a, pad)

def _compress(k, w, pe):
    B, L = k.shape[:2]
    nc = L // L_CMP
    kb = k[:, :nc * L_CMP].reshape(B, nc, L_CMP, KVH, HD) + pe[None, None, :, None, :]
    return jnp.einsum('bnpgd,pde->bnge', kb, w)

def _nsa_attend(q, kc, vc, ks, vs, kw, vw, gates, qpos0, kwpos0):
    B, Sq = q.shape[:2]
    L = ks.shape[1]
    nc = kc.shape[1]
    ns = -(-L // L_SEL)
    n_top = min(N_SEL, ns)
    pad = ns * L_SEL - L
    ks_b = jnp.pad(ks, ((0, 0), (0, pad), (0, 0), (0, 0))).reshape(B, ns, L_SEL, KVH, HD).transpose(0, 3, 1, 2, 4)
    vs_b = jnp.pad(vs, ((0, 0), (0, pad), (0, 0), (0, 0))).reshape(B, ns, L_SEL, KVH, HD).transpose(0, 3, 1, 2, 4)
    kw_p = jnp.pad(kw, ((0, 0), (WINDOW, 0), (0, 0), (0, 0)))
    vw_p = jnp.pad(vw, ((0, 0), (WINDOW, 0), (0, 0), (0, 0)))
    qb = Q_BLOCK if Sq % Q_BLOCK == 0 else Sq
    nb = Sq // qb
    span = WINDOW + qb - 1
    q_blk = q.reshape(B, nb, qb, KVH, HPG, HD).transpose(1, 0, 2, 3, 4, 5)
    g_blk = gates.reshape(B, nb, qb, KVH, HPG, 3).transpose(1, 0, 2, 3, 4, 5)
    cmp_end = jnp.arange(nc, dtype=jnp.int32) * L_CMP + (L_CMP - 1)
    blk_ids = jnp.arange(ns, dtype=jnp.int32)
    b_idx = jnp.arange(B)[:, None, None, None]
    g_idx = jnp.arange(KVH)[None, None, :, None]
    scale = HD ** -0.5

    def block(args):
        qi, gt, i = args
        t = qpos0 + i * qb + jnp.arange(qb, dtype=jnp.int32)
        s_c = jnp.einsum('bqgrd,bngd->bqgrn', qi, kc) * scale
        m_c = (cmp_end[None, :] <= t[:, None])[None, :, None, None, :]
        p_c = _masked_softmax(s_c, m_c, (-1,))
        o_c = jnp.einsum('bqgrn,bngd->bqgrd', p_c.astype(vc.dtype), vc)
        imp = jnp.pad(jnp.sum(p_c, axis=3), ((0, 0), (0, 0), (0, 0), (0, ns * (L_SEL // L_CMP) - nc)))
        imp = imp.reshape(B, qb, KVH, ns, L_SEL // L_CMP).sum(-1)
        cur = (t // L_SEL)[:, None]
        forced = (blk_ids[None] == 0) | (blk_ids[None] == cur) | (blk_ids[None] == cur - 1)
        valid = blk_ids[None] * L_SEL <= t[:, None]
        score = jnp.where(valid[None, :, None, :], imp + jnp.where(forced, FORCE_BONUS, 0.0)[None, :, None, :], -FORCE_BONUS)
        _, idx = lax.top_k(score, n_top)
        k_sel = ks_b[b_idx, g_idx, idx]
        v_sel = vs_b[b_idx, g_idx, idx]
        s_s = jnp.einsum('bqgrd,bqgksd->bqgrks', qi, k_sel) * scale
        kpos = idx[..., None] * L_SEL + jnp.arange(L_SEL, dtype=jnp.int32)
        m_s = (kpos <= t[None, :, None, None, None])[:, :, :, None]
        p_s = _masked_softmax(s_s, m_s, (-2, -1))
        o_s = jnp.einsum('bqgrks,bqgksd->bqgrd', p_s.astype(v_sel.dtype), v_sel)
        start = qpos0 + i * qb + 1 - kwpos0
        k_w = lax.dynamic_slice_in_dim(kw_p, start, span, axis=1)
        v_w = lax.dynamic_slice_in_dim(vw_p, start, span, axis=1)
        wpos = (kwpos0 - WINDOW) + start + jnp.arange(span, dtype=jnp.int32)
        m_w = ((wpos[None] >= kwpos0) & (wpos[None] <= t[:, None]) & (wpos[None] > t[:, None] - WINDOW))[None, :, None, None, :]
        s_w = jnp.einsum('bqgrd,bkgd->bqgrk', qi, k_w) * scale
        p_w = _masked_softmax(s_w, m_w, (-1,))
        o_w = jnp.einsum('bqgrk,bkgd->bqgrd', p_w.astype(v_w.dtype), v_w)
        return gt[..., 0:1] * o_c + gt[..., 1:2] * o_s + gt[..., 2:3] * o_w

    o = lax.map(block, (q_blk, g_blk, jnp.arange(nb, dtype=jnp.int32)))
    return o.transpose(1, 0, 2, 3, 4, 5).reshape(B, Sq, H_A * HD)

def _nsa_conv_mixer(x, pos0, wb, past_kv, win_past, conv_past, w_in, w_ck, pe_ck, w_cv, pe_cv,
                    conv_w, conv_b, cln_g, cln_b, w_out):
    B, S, _ = x.shape
    h = x @ w_in
    cuts = [Q_COLS + i * KV_COLS for i in range(7)] + [Q_COLS + 6 * KV_COLS + GATE_COLS,
                                                        Q_COLS + 6 * KV_COLS + GATE_COLS + C_B]
    q, kc, vc, ks, vs, kw, vw, gl, ga, gb = jnp.split(h, cuts, axis=-1)
    pos = pos0 + jnp.arange(S, dtype=jnp.int32)
    q = _rope(q.reshape(B, S, H_A, HD), pos)
    ks = _rope(ks.reshape(B, S, KVH, HD), pos)
    kw = _rope(kw.reshape(B, S, KVH, HD), pos)
    kv_rows = jnp.stack([kc.reshape(B, S, KVH, HD), vc.reshape(B, S, KVH, HD), ks,
                         vs.reshape(B, S, KVH, HD)], axis=2)
    kv_all = kv_rows if past_kv is None else jnp.concatenate([past_kv, kv_rows], axis=1)
    k_cmp = _compress(kv_all[:, :, 0], w_ck, pe_ck)
    v_cmp = _compress(kv_all[:, :, 1], w_cv, pe_cv)
    k_cmp = _rope(k_cmp, jnp.arange(k_cmp.shape[1], dtype=jnp.int32) * L_CMP + (L_CMP - 1))
    win_rows = jnp.stack([kw, vw.reshape(B, S, KVH, HD)], axis=2)
    if win_past is None:
        win_all, kwpos0 = win_rows, pos0
    else:
        win_all, kwpos0 = jnp.concatenate([win_past, win_rows], axis=1), pos0 - win_past.shape[1]
    gates = jax.nn.sigmoid(gl.reshape(B, S, H_A, 3))
    o_a = _nsa_attend(q, k_cmp, v_cmp, kv_all[:, :, 2], kv_all[:, :, 3],
                      win_all[:, :, 0], win_all[:, :, 1], gates, pos0, kwpos0)
    u = ga * jax.nn.sigmoid(gb)
    hist = jnp.zeros((B, CONV_W - 1, C_B), u.dtype) if conv_past is None else conv_past
    ue = jnp.concatenate([hist, u], axis=1)
    c = lax.conv_general_dilated(ue, conv_w[:, None, :].astype(ue.dtype), (1,), 'VALID',
                                 dimension_numbers=('NWC', 'WIO', 'NWC'), feature_group_count=C_B) + conv_b
    c = jax.nn.silu(_layer_norm(c, cln_g, cln_b))
    out = jnp.concatenate([o_a, c], axis=-1) @ w_out
    return out, kv_rows, _last_rows(win_all, wb), ue[:, ue.shape[1] - (CONV_W - 1):]

def _pool_mixer(x, pos0, pool_past, w_in, w_grp, scale, w_out):
    B, S, _ = x.shape
    u = x @ w_in
    hist = jnp.zeros((B, POOL_HIST, D_C), u.dtype) if pool_past is None else pool_past
    ue = jnp.concatenate([hist, u], axis=1)
    cs = jnp.cumsum(ue.astype(jnp.float32), axis=1)
    cs = jnp.concatenate([jnp.zeros((B, 1, D_C), jnp.float32), cs], axis=1)
    pos = pos0 + jnp.arange(S, dtype=jnp.int32)
    upper = cs[:, POOL_HIST + 1:]
    means = []
    for g, w in enumerate(POOL_WINDOWS):
        lo = POOL_HIST + 1 - w
        sl = slice(g * G_C, (g + 1) * G_C)
        cnt = jnp.minimum(pos + 1, w).astype(jnp.float32)[None, :, None]
        means.append((upper[:, :, sl] - cs[:, lo:lo + S, sl]) / cnt)
    d = jnp.concatenate(means, axis=-1) - u.astype(jnp.float32)
    d = d.astype(x.dtype).reshape(B, S, N_POOL_GROUPS, G_C)
    z = jnp.einsum('bsgc,gce->bsge', d, w_grp).reshape(B, S, D_C) * scale
    return z @ w_out, ue[:, ue.shape[1] - POOL_HIST:]

def _swiglu(x, w1, w3, w2):
    return (jax.nn.silu(x @ w1) * (x @ w3)) @ w2

def _trunk(x, pos0, wb, cache_kv, page_table, state_win, state_conv, state_pool, p):
    B = x.shape[0]
    kv_new, win_new, conv_new, pool_new = [], [], [], []
    for l in range(DEPTH):
        if l % 2 == 0:
            ia = l // 2
            if cache_kv is None:
                past_kv, win_past, conv_past = None, None, None
            else:
                past_kv = cache_kv[ia, page_table].reshape(B, -1, 4, KVH, HD)
                win_past, conv_past = state_win[ia], state_conv[ia]
            h, kv_n, win_n, conv_n = _nsa_conv_mixer(
                x, pos0, wb, past_kv, win_past, conv_past,
                p['w_in_a'][ia], p['w_cmp_k'][ia], p['pe_cmp_k'][ia], p['w_cmp_v'][ia], p['pe_cmp_v'][ia],
                p['conv_w'][ia], p['conv_b'][ia], p['conv_ln_g'][ia], p['conv_ln_b'][ia], p['w_out_a'][ia])
            kv_new.append(kv_n)
            win_new.append(win_n)
            conv_new.append(conv_n)
        else:
            ic = l // 2
            pool_past = None if state_pool is None else state_pool[ic]
            h, pool_n = _pool_mixer(x, pos0, pool_past, p['w_in_c'][ic], p['w_grp_c'][ic],
                                    p['scale_c'][ic], p['w_out_c'][ic])
            pool_new.append(pool_n)
        x = _layer_norm(ALPHA * x + h, p['ln1_g'][l], p['ln1_b'][l])
        x = _layer_norm(ALPHA * x + _swiglu(x, p['w1'][l], p['w3'][l], p['w2'][l]), p['ln2_g'][l], p['ln2_b'][l])
    return x, jnp.stack(kv_new), jnp.stack(win_new), jnp.stack(conv_new), jnp.stack(pool_new)

def setup_inputs(seed: int = 0) -> dict:
    key = jax.random.key(seed)
    k = jax.random.split(key, 32)
    n_pages = PAST_LEN // PAGE_SIZE
    n_used = DEC_BATCH * n_pages
    n_pool = n_used + max(1, n_used // 4)
    wb = min(WINDOW, PAST_LEN)

    def nrm(kk, shape, s=1.0):
        return jax.random.normal(kk, shape, jnp.float32) * s

    page_table = jax.random.permutation(k[0], n_pool)[:n_used].reshape(DEC_BATCH, n_pages).astype(jnp.int32)
    return {
        'x_prompt': nrm(k[1], (BATCH, SEQ, D_MODEL)),
        'x_sample': nrm(k[2], (DEC_BATCH, DEC_SEQ, D_MODEL)),
        'cache_kv': nrm(k[3], (N_A, n_pool, PAGE_SIZE, 4, KVH, HD)),
        'state_win': nrm(k[4], (N_A, DEC_BATCH, wb, 2, KVH, HD)),
        'state_conv': nrm(k[5], (N_A, DEC_BATCH, CONV_W - 1, C_B), 0.5),
        'state_pool': nrm(k[6], (N_C, DEC_BATCH, POOL_HIST, D_C)),
        'page_table': page_table,
        'w_in_a': nrm(k[7], (N_A, D_MODEL, IN_A), D_MODEL ** -0.5),
        'w_cmp_k': nrm(k[8], (N_A, L_CMP, HD, HD), (L_CMP * HD) ** -0.5),
        'pe_cmp_k': nrm(k[9], (N_A, L_CMP, HD), 0.1),
        'w_cmp_v': nrm(k[10], (N_A, L_CMP, HD, HD), (L_CMP * HD) ** -0.5),
        'pe_cmp_v': nrm(k[11], (N_A, L_CMP, HD), 0.1),
        'conv_w': nrm(k[12], (N_A, CONV_W, C_B), CONV_W ** -0.5),
        'conv_b': nrm(k[13], (N_A, C_B), 0.01),
        'conv_ln_g': 1.0 + nrm(k[14], (N_A, C_B), 0.02),
        'conv_ln_b': nrm(k[15], (N_A, C_B), 0.01),
        'w_out_a': nrm(k[16], (N_A, OUT_A, D_MODEL), BETA * OUT_A ** -0.5),
        'w_in_c': nrm(k[17], (N_C, D_MODEL, D_C), D_MODEL ** -0.5),
        'w_grp_c': nrm(k[18], (N_C, N_POOL_GROUPS, G_C, G_C), G_C ** -0.5),
        'scale_c': 1.0 + nrm(k[19], (N_C, D_C), 0.02),
        'w_out_c': nrm(k[20], (N_C, D_C, D_MODEL), BETA * D_C ** -0.5),
        'ln1_g': 1.0 + nrm(k[21], (DEPTH, D_MODEL), 0.02),
        'ln1_b': nrm(k[22], (DEPTH, D_MODEL), 0.01),
        'ln2_g': 1.0 + nrm(k[23], (DEPTH, D_MODEL), 0.02),
        'ln2_b': nrm(k[24], (DEPTH, D_MODEL), 0.01),
        'w1': nrm(k[25], (DEPTH, D_MODEL, D_FF), D_MODEL ** -0.5),
        'w3': nrm(k[26], (DEPTH, D_MODEL, D_FF), D_MODEL ** -0.5),
        'w2': nrm(k[27], (DEPTH, D_FF, D_MODEL), BETA * D_FF ** -0.5),
    }

def reference(x_prompt, x_sample, cache_kv, state_win, state_conv, state_pool, page_table,
              w_in_a, w_cmp_k, pe_cmp_k, w_cmp_v, pe_cmp_v, conv_w, conv_b, conv_ln_g, conv_ln_b,
              w_out_a, w_in_c, w_grp_c, scale_c, w_out_c, ln1_g, ln1_b, ln2_g, ln2_b, w1, w3, w2):
    p = dict(w_in_a=w_in_a, w_cmp_k=w_cmp_k, pe_cmp_k=pe_cmp_k, w_cmp_v=w_cmp_v, pe_cmp_v=pe_cmp_v,
             conv_w=conv_w, conv_b=conv_b, conv_ln_g=conv_ln_g, conv_ln_b=conv_ln_b, w_out_a=w_out_a,
             w_in_c=w_in_c, w_grp_c=w_grp_c, scale_c=scale_c, w_out_c=w_out_c,
             ln1_g=ln1_g, ln1_b=ln1_b, ln2_g=ln2_g, ln2_b=ln2_b, w1=w1, w3=w3, w2=w2)
    wb = state_win.shape[2]
    past_len = page_table.shape[1] * cache_kv.shape[2]
    y_prompt, kv_prompt, win_prompt, conv_prompt, pool_prompt = _trunk(
        x_prompt, 0, wb, None, None, None, None, None, p)
    y_sample, kv_sample, win_sample, conv_sample, pool_sample = _trunk(
        x_sample, past_len, wb, cache_kv, page_table, state_win, state_conv, state_pool, p)
    return (y_prompt, y_sample, kv_prompt, kv_sample, win_prompt, win_sample,
            conv_prompt, conv_sample, pool_prompt, pool_sample)


_drawn_inputs = setup_inputs


def setup_inputs(seed=0):
    import zlib

    import numpy as np

    out = dict(_drawn_inputs(seed))
    spreads = {}
    factors = {'pe_cmp_k': 81.185,
     'pe_cmp_v': 20.309,
     'conv_b': 8.0,
     'conv_ln_g': 74.901,
     'conv_ln_b': 147.904,
     'scale_c': 67.724,
     'ln1_b': 3.849,
     'ln2_b': 4.003,
     'cache_kv': 3.463,
     'w_cmp_k': 3.121,
     'w_cmp_v': 2.78}
    for name, (base, spread) in spreads.items():
        noise = np.random.default_rng([zlib.crc32(name.encode()), seed]).standard_normal(out[name].shape)
        drawn = base * np.exp(spread * noise) if base else spread * noise
        out[name] = __import__('jax').numpy.asarray(drawn.astype(out[name].dtype))
    for name, factor in factors.items():
        out[name] = (out[name] * factor).astype(out[name].dtype)
    return out
```

```python
from contextlib import ExitStack

import concourse.bass as bass
from concourse import mybir

F32 = mybir.dt.float32
F32R = mybir.dt.float32r
I32 = mybir.dt.int32
ACT = mybir.ActivationFunctionType
ALU = mybir.AluOpType
AX = mybir.AxisListType

P = 128
D = 1024
KT = D // P
NP_TOK = 1024
SB, SS = 8, 8
T = NP_TOK + SB * SS
CH = 364
NCH = 3
TP = CH * NCH
LAST = NP_TOK - 2 * CH
HD, G, R = 64, 2, 4
QT_N = NP_TOK // P
CW = 31
CT = 4
UEP = CW - 1 + NP_TOK
UES = CW - 1 + SS
UEW = UEP + SB * UES
FT = 22
FG = FT // 2
NB = 32
PAGES = 8
NPOOL = 80
BIG = 1.0e30
TINY = 1.0e-30
EPS = 1e-5
SCALE = HD ** -0.5
ALPHA = 4 ** 0.25
TAKEN = -3.0e38
W_HIST = 512
PH = 15
PUP = PH + NP_TOK
PUS = PH + SS
PUW = PUP + SB * PUS

IN_ORDER = ["ks", "kw", "gb0", "ga0", "kc", "vc", "vs", "gb1", "ga1", "vw", "gb2", "ga2",
            "q0", "q1", "gb3", "ga3", "q2", "q3", "gl"]
KV_AT = {"kc": 0, "vc": 1, "ks": 2, "vs": 3, "kw": 4, "vw": 5}
N_IN = len(IN_ORDER)
N_FFN = 3 * FT
AT_IN, AT_OUT = 0, N_IN
AT_F0 = AT_OUT + KT
AT_INC = AT_F0 + N_FFN
AT_GRP = AT_INC + KT
AT_OUTC = AT_GRP + 2
AT_F1 = AT_OUTC + KT
N_W = AT_F1 + N_FFN
RING = 3
EARLY = 24
assert N_W % RING == 0 and EARLY % RING == 0

PR_CW, PR_CB, PR_CG, PR_CN = 0, CT * CW, CT * CW + 4, CT * CW + 8
PR_SC = PR_CN + 4
PR_LN = PR_SC + 8
PR_N = PR_LN + 64
AC_CAUS, AC_WM = 0, P
AC_CMA = AC_WM + 640
AC_CMM = AC_CMA + QT_N * NB
AC_SB = AC_CMM + QT_N * NB
AC_N = AC_SB + QT_N * 16
SC_G, SC_WM = 0, P
SC_NEW = SC_WM + W_HIST + SS
SC_SB = SC_NEW + SS
SC_COS = SC_SB + 17
SC_SIN = SC_COS + NB * (1 + SB)
SC_N = SC_SIN + NB * (1 + SB) + 3


def build(nc, xT, wst, params, consts, att_c, smp_c, cosT, sinT, pe_t, cw_k, cw_v, hist_c, hist_p, invc,
          cache, swk, swv, win_past, ptab, yT, kvT, win_old, convT, poolT):
    ctx = ExitStack()
    base = [16512]

    def place(name, shape, dt, at):
        return nc.alloc_sbuf_tensor_at(name, shape, dt, offset=at)

    def size(*dims):
        n = 4
        for d in dims:
            n *= d
        return -(-n // 32) * 32

    def region(n):
        at = base[0]
        base[0] += n
        return at

    r_x = region(2 * size(KT, TP))
    r_y = region(size(KT, TP))
    r_w = region(3 * size(RING, 1024))
    r_c = region(size(3 * P) + size(PR_N))
    r_f = base[0]
    end = nc.sbuf_usable_end

    XH = place("XH", [P, KT, TP], F32R, r_x)
    XL = place("XL", [P, KT, TP], F32R, r_x + size(KT, TP))
    XHf, XLf = XH[:, :, :].bitcast(F32), XL[:, :, :].bitcast(F32)
    Y = place("Y", [P, KT, TP], F32, r_y)
    XRAW = place("XRAW", [P, KT, TP], F32, r_y)
    RAW = place("RAW", [P, RING, 1024], F32, r_w)
    WH = place("WH", [P, RING, 1024], F32R, r_w + size(RING, 1024))
    WL = place("WL", [P, RING, 1024], F32R, r_w + 2 * size(RING, 1024))
    CST = place("CST", [P, 3, P], F32, r_c)
    PR = place("PR", [P, PR_N], F32, r_c + size(3 * P))
    ident, ones_d, ones_c = CST[:, 0, :], CST[:, 1, :], CST[:, 2, :]

    QT = place("QT", [P, R, TP], F32, r_y)
    KV4 = place("KV4", [P, 4, TP], F32, r_y + size(R, TP))
    KV2 = place("KV2", [P, 2, TP], F32, r_f)
    CA = place("CA", [P, CT, TP], F32, r_f + size(2, TP))
    r_u = r_f + size(2, TP) + size(CT, TP)
    UE = place("UE", [P, CT, UEW], F32, r_u)
    r_t = r_u + size(CT, UEW)
    COS = place("COS", [P, TP], F32, r_t)
    SIN = place("SIN", [P, TP], F32, r_t + size(TP))
    ROT = place("ROT", [P, TP], F32, r_t + 2 * size(TP))
    SG = place("SG", [P, TP], F32, r_t + 3 * size(TP))
    GT = place("GT", [24, TP], F32, r_t + 3 * size(TP))
    PTAB = place("PTAB", [1, 64], I32, r_t + 4 * size(TP))
    GN = place("GN", [P, QT_N, 24], F32, r_t + 4 * size(TP) + 256)
    GNS = place("GNS", [P, 4, 3], F32, r_t + 4 * size(TP) + 256 + size(QT_N * 24))
    MS = place("MS", [P, R, SB * SS], F32, r_t + 4 * size(TP) + 256 + size(QT_N * 24) + 64)
    PEC = place("PEC", [P, 2, NB], F32, r_t + 4 * size(TP) + 256 + size(QT_N * 24) + 64 + 1024)
    assert 256 + r_t + 4 * size(TP) + 256 + size(QT_N * 24) + 64 + 1024 <= end

    def kv(name):
        i = KV_AT[name]
        return KV4[:, i, :] if i < 4 else KV2[:, i - 4, :]

    PG = place("PG", [P, 2, 32, P], F32, r_x)
    CWK = place("CWK", [P, 32, P], F32, r_x + size(64, P))
    CWV = place("CWV", [P, 32, P], F32, r_x + size(96, P))
    g_bytes = size(16, 256) + size(2, 512) + size(2, 512)
    KVP = [place(f"KVP{i}", [P, 16, 2, P], F32, r_x + i * g_bytes) for i in range(2)]
    KWS = [place(f"KWS{i}", [P, 2, W_HIST], F32, r_x + i * g_bytes + size(16, 256)) for i in range(2)]
    VWS = [place(f"VWS{i}", [P, 2, 4, P], F32, r_x + i * g_bytes + size(16, 256) + size(2, 512)) for i in range(2)]
    VN = place("VN", [SS, 2, SB, P], F32, r_x + 2 * g_bytes)
    VCS = place("VCS", [NB, SB, P], F32, r_x + 2 * g_bytes + size(16, P))
    SMC = place("SMC", [P, SC_N], F32, r_x + 2 * g_bytes + size(24, P))
    assert 2 * g_bytes + size(24, P) + size(SC_N) <= 2 * size(KT, TP)
    VNAT = place("VNAT", [P, 2, QT_N, P], F32, r_y + size(R, TP))
    a = [r_u]

    def scratch(name, shape, dt=F32):
        t = place(name, shape, dt, a[0])
        a[0] += size(*shape[1:])
        return t

    ATC = scratch("ATC", [P, AC_N])
    KCT = scratch("KCT", [P, NB * (1 + SB)])
    VBD = scratch("VBD", [P, G, R * HD])
    QS = scratch("QS", [P, SB, R, SS])
    pb_at = a[0]
    PB = scratch("PB", [P, 2, 1056])
    PTB = scratch("PTB", [P, 2, 8 * P])
    SMASK = scratch("SMASK", [P, 1024])
    OC = scratch("OC", [P, R, G, HD])
    OTMP = scratch("OTMP", [P, R * HD])
    ST = scratch("ST", [P, 288])
    assert a[0] <= r_t + 3 * size(TP), (a[0], r_t)
    KR = place("KR", [P, 2, NB * (1 + SB)], F32, a[0] - size(288) - size(256) - size(512) - size(1024))

    f = [r_f]

    def ffn_t(name, shape, dt=F32):
        t = place(name, shape, dt, f[0])
        f[0] += size(*shape[1:])
        return t

    HH = ffn_t("HH", [P, 2, TP], F32R)
    HL = ffn_t("HL", [P, 2, TP], F32R)
    HHf = HH[:, :, :].bitcast(F32)
    SL = ffn_t("SL", [P, TP])
    HT = ffn_t("HT", [P, 2, TP])
    SQ = ffn_t("SQ", [P, KT, CH])
    RS = ffn_t("RS", [P, CH])
    assert f[0] <= end
    UP = place("UP", [P, KT, PUW], F32, r_f)
    s_at = r_f + size(KT, PUW)
    SUM = place("SUM", [P, 2, PUW], F32, s_at)
    POUT = place("POUT", [P, KT, 9, PH], F32, s_at + size(2, PUW))
    INV = place("INV", [P, 4, 16], F32, s_at + size(2, PUW) + size(KT, 9, PH))
    assert s_at + size(2, PUW) + size(KT, 9, PH) + 256 <= end
    SQC = place("SQC", [P, CT, CH], F32, pb_at)
    RSC = place("RSC", [P, CH], F32, pb_at + size(CT, CH))

    gsc = nc.dram_tensor("gate_bounce", (SB * SS, 24), F32, kind="Internal").ap()

    with ctx:
        PS = ctx.enter_context(nc.psum_tensor("PS", [P, 8, 512], F32))

        def sem(name):
            return ctx.enter_context(nc.semaphore(name))

        raw_loaded = [sem(f"raw_loaded{i}") for i in range(RING)]
        hi_done, pool_turn = sem("hi_done"), sem("pool_turn")
        w_split = sem("w_split")
        w_free = sem("w_free")
        c_loaded = sem("c_loaded")
        x_loaded = sem("x_loaded")
        x_hi = sem("x_hi")
        x_split = sem("x_split")
        full = {s: sem(f"full_{s}") for s in ("in", "out", "f0", "inc", "grp", "outc", "f1")}
        free = {s: sem(f"free_{s}") for s in ("in", "out", "inc", "grp", "outc")}
        set_free = {s: [sem(f"set_free_{s}_{q}") for q in range(2)] for s in ("f0", "f1")}
        hist_loaded = sem("hist_loaded")
        ue_zeroed = sem("ue_zeroed")
        rot_full, rot_free = sem("rot_full"), sem("rot_free")
        sg_full, sg_free, ga_full = sem("sg_full"), sem("sg_free"), sem("ga_full")
        kv_evac = sem("kv_evac")
        roped = sem("roped")
        gated = sem("gated")
        conv_step = sem("conv_step")
        dv = sem("dv")
        gl_done = sem("gl_done")
        kv_stored = sem("kv_stored")
        cw_loaded = [sem("cw_loaded_k"), sem("cw_loaded_v")]
        pg_loaded = [sem("pg_loaded0"), sem("pg_loaded1")]
        pe_loaded, vbd_in = sem("pe_loaded"), sem("vbd_in")
        job_done = sem("job_done")
        cmp_acc = sem("cmp_acc")
        att_c_loaded = sem("att_c_loaded")
        smp_c_loaded = sem("smp_c_loaded")
        kr_done = sem("kr_done")
        turned, turned_out = sem("turned"), sem("turned_out")
        kct_done = sem("kct_done")
        vbd_zero = sem("vbd_zero")
        g_out, g_in = sem("g_out"), sem("g_in")
        sp_loaded = [sem("sp_loaded0"), sem("sp_loaded1")]
        s_cmp, s_win, s_sel = sem("s_cmp"), sem("s_win"), sem("s_sel")
        s_pc, s_imp = sem("s_pc"), sem("s_imp")
        s_cexp_in, s_cexp = sem("s_cexp_in"), sem("s_cexp")
        s_masked, s_exp = sem("s_masked"), sem("s_exp")
        s_turn, s_turned = sem("s_turn"), sem("s_turned")
        s_pv, s_mixed, s_outT, s_ms = sem("s_pv"), sem("s_mixed"), sem("s_outT"), sem("s_ms")
        ms_hi = sem("ms_hi")
        ln_in, ln_mean, ln_cent, ln_sq = sem("ln_in"), sem("ln_mean"), sem("ln_cent"), sem("ln_sq")
        ln_var, ln_ve, ln_sqrt, ln_norm, ln_hi, ln_x = (sem("ln_var"), sem("ln_ve"), sem("ln_sqrt"), sem("ln_norm"),
                                                 sem("ln_hi"), sem("ln_x"))
        cv_act = sem("cv_act")
        p_scores, p_masked, p_exp = sem("p_scores"), sem("p_masked"), sem("p_exp")
        p_cin, p_cexp = sem("p_cin"), sem("p_cexp")
        p_t0, p_t1, p_c0, p_c1 = sem("p_t0"), sem("p_t1"), sem("p_c0"), sem("p_c1")
        p_pv, p_mixed = sem("p_pv"), sem("p_mixed")
        p_ot, p_ohi, p_olo = sem("p_ot"), sem("p_ohi"), sem("p_olo")
        silu_done = [sem("silu_done0"), sem("silu_done1")]
        ht_done = [sem("ht_done0"), sem("ht_done1")]
        hh_done = [sem("hh_done0"), sem("hh_done1")]
        hl_done = [sem("hl_done0"), sem("hl_done1")]
        y_full = [sem("y_full0"), sem("y_full1")]
        y_free = [sem("y_free0"), sem("y_free1")]
        x_again = sem("x_again")
        up_zero, up_in, d_done, dh_done, dl_done, zh_done, zl_done = (
            sem("up_zero"), sem("up_in"), sem("d_done"), sem("dh_done"), sem("dl_done"), sem("zh_done"), sem("zl_done"))
        hp_loaded = sem("hp_loaded")
        inv_loaded = sem("inv_loaded")
        stored = sem("stored")

        N_PROMPT_UNITS = []
        for i in range(QT_N):
            for g in range(G):
                N_PROMPT_UNITS.append((i, g, "cmp", 0, 0, 1))
                for r in range(R):
                    N_PROMPT_UNITS.append((i, g, "win", r, max(0, i - 4), min(i + 1, 5)))
                for r in range(R):
                    N_PROMPT_UNITS.append((i, g, "sel", r, 0, i + 1))
        units = N_PROMPT_UNITS
        first = [min(4, -(-u[5] // 2)) if u[5] > 1 else 1 for u in units]
        t1_upto = [0]
        for u, n in zip(units, first):
            t1_upto.append(t1_upto[-1] + (u[5] > n))
        big = [n for n, u in enumerate(units) if u[2] != "cmp"]
        big_upto = [0]
        for u in units:
            big_upto.append(big_upto[-1] + (u[2] != "cmp"))
        last_of = {(u[0], u[1]): n for n, u in enumerate(units)}
        N_STORES = []
        block = ctx.enter_context(nc.Block())

        def turns():
            for k, name in enumerate(("vs", "vw")):
                for h in range(2):
                    yield [(kv(name)[:, (4 * h + j) * P:(4 * h + j + 1) * P], P, P) for j in range(4)], \
                        VNAT[:, k, 4 * h:4 * h + 4, :], P
            for k, name in enumerate(("vs", "vw")):
                for h in range(2):
                    yield [(kv(name)[:, NP_TOK + (4 * h + j) * SS:NP_TOK + (4 * h + j + 1) * SS], P, SS)
                           for j in range(4)], VN[:, k, 4 * h:4 * h + 4, :], SS
            for h in range(2):
                yield [(KR[:, 1, NB * (1 + 4 * h + j):NB * (2 + 4 * h + j)], P, NB) for j in range(4)], \
                    VCS[:, 4 * h:4 * h + 4, :], NB

        TURNS = list(turns())
        T_GATE, T_VBD = len(TURNS), len(TURNS) + 1
        N_TURNS = len(TURNS) + 2

        @block.sync
        def _(sp):
            sp.dma_start(CST[:, :, :], consts).then_inc(c_loaded, 16)
            sp.dma_start(PR[:, :], params).then_inc(c_loaded, 16)
            for k in range(KT):
                sp.dma_start(XRAW[:, k, :], xT[k]).then_inc(x_loaded, 16)
            sp.dma_start(COS[:, :], cosT).then_inc(c_loaded, 16)
            sp.dma_start(SIN[:, :], sinT).then_inc(c_loaded, 16)
            for c in range(CT):
                sp.dma_start(UE[:, c, UEP:].rearrange("p (b u) -> p b u", b=SB)[:, :, 0:CW - 1],
                             hist_c[:, c]).then_inc(hist_loaded, 16)
            sp.dma_start(PTAB[:, :], ptab).then_inc(c_loaded, 16)

            def weights(start, n):
                with sp.Fori(0, n // RING) as it:
                    for s in range(RING):
                        sp.wait_ge(w_split, it * RING + start + s + 1)
                        sp.dma_start(RAW[:, s, :], wst[bass.ds(it * RING + start + s, 1), :, :]
                                     .rearrange("a p n -> (a p) n")).then_inc(raw_loaded[s], 16)

            weights(0, EARLY)
            sp.wait_ge(c_loaded, 5 * 16)
            sp.wait_ge(full["in"], N_IN)
            sp.dma_start(CWK[:, :, :], cw_k).then_inc(cw_loaded[0], 16)
            for job in range(4):
                if job >= 2:
                    sp.wait_ge(job_done, job - 1)
                kind, half = job // 2, job % 2
                with sp.Fori(0, 32) as i:
                    page = sp.value_load(PTAB[0:1, bass.ds(i + 32 * half, 1)], min_val=0, max_val=NPOOL - 1)
                    sp.dma_start(PG[:, half, bass.ds(i, 1), :].rearrange("p a n -> p (a n)"),
                                 cache[bass.ds(page, 1), :, kind, :].rearrange("a p n -> (a p) n")
                                 ).then_inc(pg_loaded[half], 16)
                if job == 0:
                    sp.dma_start(CWV[:, :, :], cw_v).then_inc(cw_loaded[1], 16)
                    sp.wait_ge(gl_done, 1)
                    sp.wait_ge(roped, 6)
                    for n in range(4):
                        sp.dma_start(kvT[n], KV4[:, n, :]).then_inc(kv_stored, 16)
                    for n in range(2):
                        sp.dma_start(kvT[4 + n], KV2[:, n, :]).then_inc(kv_stored, 16)
                    sp.dma_start(gsc.rearrange("t n -> n t"), GT[0:24, NP_TOK:T], allow_slow_non_contiguous=True).then_inc(g_out, 16)
                if job == 1:
                    sp.wait_ge(gated, CT)
                    sp.dma_start(convT[:, :, 0, :], UE[:, :, NP_TOK:UEP]).then_inc(kv_stored, 16)
                    for c in range(CT):
                        sp.dma_start(convT[:, c, 1:, :], UE[:, c, UEP:].rearrange("p (b u) -> p b u", b=SB)
                                     [:, :, SS:]).then_inc(kv_stored, 16)
                    sp.wait_ge(g_out, 16)
                    rows = gsc.rearrange("(gi bb s) (g r br) -> g r bb s gi br", g=G, r=R, bb=2, s=SS)
                    for bb in range(2):
                        for g in range(G):
                            for r in range(R):
                                at = 32 * (2 * bb + g) + r * SS
                                sp.dma_start(GNS[at:at + SS, :, :], rows[g, r, bb]).then_inc(g_in, 16)
            sp.wait_ge(conv_step, 2 * CW * CT)
            sp.wait_ge(roped, 6)
            sp.wait_ge(kv_stored, 11 * 16)
            sp.dma_start(ATC[:, :], att_c).then_inc(att_c_loaded, 16)
            sp.wait_ge(job_done, 4)
            sp.dma_start(SMC[:, :], smp_c).then_inc(smp_c_loaded, 16)

            def sample_loads(gi):
                b2 = gi % 2
                with sp.Fori(0, 16) as i:
                    page = sp.value_load(PTAB[0:1, bass.ds(i + 16 * gi, 1)], min_val=0, max_val=NPOOL - 1)
                    sp.dma_start(KVP[b2][:, bass.ds(i, 1), :, :].rearrange("p a k n -> p (a k n)"),
                                 cache[bass.ds(page, 1), :, 2:4, :].rearrange("a p k n -> (a p) (k n)")
                                 ).then_inc(sp_loaded[b2], 16)
                sp.dma_start(KWS[b2][:, :, :], swk[2 * gi:2 * gi + 2].rearrange("b p n -> p b n")).then_inc(sp_loaded[b2], 16)
                sp.dma_start(VWS[b2][:, :, :, :], swv[2 * gi:2 * gi + 2].rearrange("b p k n -> p b k n")).then_inc(sp_loaded[b2], 16)

            for gi in range(4):
                if gi >= 2:
                    sp.wait_ge(s_pv, 3 * (gi - 1))
                sample_loads(gi)
            sp.dma_start(win_old, win_past).then_inc(stored, 16)
            sp.wait_ge(p_pv, len(units))
            for k in range(KT):
                sp.dma_start(Y[:, k, :], xT[k]).then_inc(x_again, 16)
            weights(EARLY, N_W - EARLY)

        @block.gpsimd
        def _(pool):
            pool.sem_inc(w_split, RING)
            with pool.Fori(0, N_W // RING) as it:
                for s in range(RING):
                    pool.wait_ge(raw_loaded[s], it * 16 + 16)
                    pool.wait_ge(w_free, it * RING + s + 1)
                    pool.sem_inc(pool_turn, 1)
                    pool.tensor_copy(WH[:, s, :], RAW[:, s, :]).then_inc(hi_done, 1)
                    pool.wait_ge(hi_done, it * RING + s + 1)
                    pool.tensor_tensor(WL[:, s, :], RAW[:, s, :], WH[:, s, :].bitcast(F32),
                                       ALU.subtract).then_inc(w_split, 1)

        @block.tensor
        def _(pe):
            pe.sem_inc(w_free, RING)

            used = [0]

            def passes(out, w, x, start, stop):
                mm = pe.matmul(out, w[0], x[0], start=start, stop=False)
                if used[0]:
                    mm.then_inc(w_free, used[0])
                    used[0] = 0
                pe.matmul(out, w[1], x[0], start=False, stop=False)
                return pe.matmul(out, w[0], x[1], start=False, stop=stop)

            def weight(s, col):
                return WH[:, s, col:col + P], WL[:, s, col:col + P]

            def tile(n, s, bank_set, st, col=0, ks=range(KT), release=True, chunk_wait=None):
                pe.wait_ge(w_split, n + (1 + RING))
                for c in range(NCH):
                    if chunk_wait:
                        chunk_wait(c)
                    for q, k in enumerate(ks):
                        mm = passes(PS[:, 3 * bank_set + c, 0:CH], weight(s, col + q * P),
                                    (XH[:, k, c * CH:(c + 1) * CH], XL[:, k, c * CH:(c + 1) * CH]),
                                    q == 0, q == len(ks) - 1)
                mm.then_inc(full[st], 1)
                if release:
                    used[0] += 1

            def project(st, n0, count, chunk_wait=None):
                loops = (count - 1) // 6
                done = 0

                def one(n, s, q, first_wait):
                    pe.wait_ge(free[st], n + 1)
                    tile(n0 + n, s, q % 2, st, chunk_wait=first_wait)

                one(0, n0 % RING, 0, chunk_wait)
                done = 1
                if loops:
                    with pe.Fori(0, loops) as it:
                        for j in range(6):
                            one(it * 6 + (1 + j), (n0 + 1 + j) % RING, 1 + j, None)
                    done += 6 * loops
                for n in range(done, count):
                    one(n, (n0 + n) % RING, n, None)

            def layer_norm(L, src, ones, nk, base_n, last_cent):
                for c in range(NCH):
                    pe.wait_ge(ln_in, base_n + c + 1)
                    for k in range(nk):
                        mm = pe.matmul(PS[:, c, 0:CH], ones, src[:, k, c * CH:(c + 1) * CH],
                                       start=(k == 0), stop=(k == nk - 1))
                    mm.then_inc(ln_mean, 1)
                sq = SQC if nk == CT else SQ
                for c in range(NCH):
                    pe.wait_ge(ln_sq, base_n + c + 1)
                    for k in range(nk):
                        mm = pe.matmul(PS[:, 3 + c, 0:CH], ones, sq[:, k, :], start=(k == 0), stop=(k == nk - 1))
                    mm.then_inc(ln_var, 1)

            pe.wait_ge(c_loaded, 5 * 16)
            pe.wait_ge(x_split, KT)
            project("in", AT_IN, N_IN)

            def compress(out, w, src):
                for p in range(NB):
                    mm = pe.matmul(out, w[:, p, :], src(p), start=(p == 0), stop=(p == NB - 1))
                return mm

            pe.wait_ge(free["in"], 2 + N_IN)
            for kind in range(2):
                w = (CWK, CWV)[kind]
                pe.wait_ge(cw_loaded[kind], 16)
                pe.wait_ge(pe_loaded, 16)
                compress(PS[:, kind, 288:289], w, lambda p: PEC[:, kind, p:p + 1])
                compress(PS[:, kind, 0:NB], w, lambda p: KV4[:, kind, 0:NP_TOK].rearrange("q (n p) -> q n p", p=NB)[:, :, p])
                for half in range(2):
                    pe.wait_ge(pg_loaded[half], 32 * 16 * (kind + 1))
                    mm = compress(PS[:, kind, NB + half * P:NB + (half + 1) * P], w,
                                  lambda p: PG[:, half, :, :].rearrange("q a (n p) -> q (a n) p", p=NB)[:, :, p])
                    mm.then_inc(job_done, 1)

            def turn_bank(n):
                return 4 + n % 2

            pe.wait_ge(kr_done, 1)
            pe.wait_ge(roped, 6)
            for n, (srcs, _, rows) in enumerate(TURNS):
                if n >= 2:
                    pe.wait_ge(turned_out, n - 1)
                for j, (src, _, _) in enumerate(srcs):
                    mm = pe.transpose(PS[0:rows, turn_bank(n), j * P:(j + 1) * P], src, ident)
                mm.then_inc(turned, 1)
            pe.wait_ge(turned_out, T_GATE - 1)
            pe.wait_ge(gl_done, 1)
            for i in range(QT_N):
                mm = pe.transpose(PS[:, turn_bank(T_GATE), i * 24:(i + 1) * 24], GT[0:24, i * P:(i + 1) * P],
                                  ident[0:24, 0:24])
            mm.then_inc(turned, 1)
            pe.wait_ge(turned_out, T_VBD - 1)
            pe.transpose(PS[0:NB, turn_bank(T_VBD), 0:P], KR[:, 1, 0:NB], ident).then_inc(turned, 1)

            pe.wait_ge(turned_out, N_TURNS)
            pe.wait_ge(kct_done, 1)
            pe.wait_ge(smp_c_loaded, 16)
            turn = 0
            for gi in range(4):
                b2 = gi % 2

                def pairs():
                    for bb in range(2):
                        for g in range(G):
                            j = 2 * bb + g
                            at = NP_TOK + (2 * gi + bb) * SS
                            yield bb, g, slice(32 * j, 32 * j + 32), slice(g * HD, g * HD + HD), \
                                QS[g * HD:g * HD + HD, 2 * gi + bb, :, :].rearrange("p r s -> p (r s)"), at

                if gi:
                    pe.wait_ge(s_ms, gi)
                for bb, g, rows, feat, q, at in pairs():
                    mm = pe.matmul(PS[rows, 5, 0:NB], q, KCT[feat, NB * (1 + 2 * gi + bb):NB * (2 + 2 * gi + bb)],
                                   start=True, stop=True)
                mm.then_inc(s_cmp, 1)
                pe.wait_ge(sp_loaded[b2], 18 * 16 * (gi // 2 + 1))
                for bb, g, rows, feat, q, at in pairs():
                    pe.matmul(PS[rows, 0, :], q, KWS[b2][feat, bb, :], start=True, stop=True)
                    mm = pe.matmul(PS[rows, 1, 0:SS], q, kv("kw")[feat, at:at + SS], start=True, stop=True)
                mm.then_inc(s_win, 1)
                for bb, g, rows, feat, q, at in pairs():
                    for h in range(2):
                        pe.matmul(PS[rows, 2 + h, :], q, KVP[b2][feat, 8 * bb + 4 * h:8 * bb + 4 * h + 4, 0, :],
                                  start=True, stop=True)
                    mm = pe.matmul(PS[rows, 4, 0:SS], q, kv("ks")[feat, at:at + SS], start=True, stop=True)
                mm.then_inc(s_sel, 1)
                pe.wait_ge(s_pc, gi + 1)
                pe.matmul(PS[:, 5, 64:64 + NB], SMC[:, SC_G:SC_G + P], ST[:, 64:64 + NB], start=True, stop=True).then_inc(s_imp, 1)

                def turned_tiles(src, cols):
                    nonlocal turn
                    if turn:
                        pe.wait_ge(s_turned, turn)
                    for n, (lo, hi) in enumerate(cols):
                        mm = pe.transpose(PS[0:hi - lo, 6, n * P:(n + 1) * P], src[:, lo:hi], ident)
                    mm.then_inc(s_turn, 1)
                    turn += 1

                turned_tiles(ST, [(64, 64 + NB)])
                pe.wait_ge(s_turned, turn)
                for bb, g, rows, feat, q, at in pairs():
                    mm = pe.matmul(PS[rows, 7, 0:HD], PTB[0:NB, 0, rows], VCS[:, 2 * gi + bb, feat], start=True, stop=True)
                mm.then_inc(s_pv, 1)
                pe.wait_ge(s_exp, 2 * gi + 1)
                turned_tiles(PB[:, 0, :], [(k * P, k * P + P) for k in range(4)])
                turned_tiles(PB[:, 0, :], [(W_HIST, W_HIST + SS)])
                pe.wait_ge(s_turned, turn)
                for bb, g, rows, feat, q, at in pairs():
                    for k in range(4):
                        pe.matmul(PS[rows, 7, HD:2 * HD], PTB[:, 0, k * P + 32 * (2 * bb + g):k * P + 32 * (2 * bb + g) + 32],
                                  VWS[b2][:, bb, k, feat], start=(k == 0), stop=False)
                    mm = pe.matmul(PS[rows, 7, HD:2 * HD], PTB[0:SS, 0, 4 * P + 32 * (2 * bb + g):4 * P + 32 * (2 * bb + g) + 32],
                                   VN[:, 1, 2 * gi + bb, feat], start=False, stop=True)
                mm.then_inc(s_pv, 1)
                pe.wait_ge(s_exp, 2 * gi + 2)
                turned_tiles(PB[:, 1, :], [(k * P, k * P + P) for k in range(4)])
                turned_tiles(PB[:, 1, :], [(k * P, k * P + P) for k in range(4, 8)])
                turned_tiles(PB[:, 1, :], [(8 * P, 8 * P + SS)])
                pe.wait_ge(s_turned, turn)
                for bb, g, rows, feat, q, at in pairs():
                    j = 32 * (2 * bb + g)
                    for k in range(8):
                        pe.matmul(PS[rows, 7, 2 * HD:3 * HD], PTB[:, k // 4, (k % 4) * P + j:(k % 4) * P + j + 32],
                                  KVP[b2][:, 8 * bb + k, 1, feat], start=(k == 0), stop=False)
                    mm = pe.matmul(PS[rows, 7, 2 * HD:3 * HD], PTB[0:SS, 0, 4 * P + j:4 * P + j + 32],
                                   VN[:, 0, 2 * gi + bb, feat], start=False, stop=True)
                mm.then_inc(s_pv, 1)
                pe.wait_ge(s_mixed, gi + 1)
                pe.transpose(PS[0:HD, 5, 128:256], OC[:, 0, 0, :], ident).then_inc(s_outT, 1)

            pe.wait_ge(s_ms, 4)
            layer_norm(0, CA, ones_c, CT, 0, None)

            def scores(n):
                i, g, kind, r, k0, nk = units[n]
                b = 2 * (n % 2)
                feat = slice(g * HD, g * HD + HD)
                if n >= 2:
                    pe.wait_ge(p_masked, n - 1)
                if kind == "cmp":
                    for h in range(R):
                        mm = pe.matmul(PS[:, b, h * NB:(h + 1) * NB], QT[feat, h, i * P:(i + 1) * P], KCT[feat, 0:NB],
                                       start=True, stop=True)
                else:
                    src = kv("ks" if kind == "sel" else "kw")
                    for h in range(-(-nk // 4)):
                        w = min(4, nk - 4 * h) * P
                        at = (k0 + 4 * h) * P
                        mm = pe.matmul(PS[:, b + h, 0:w], QT[feat, r, i * P:(i + 1) * P], src[feat, at:at + w],
                                       start=True, stop=True)
                mm.then_inc(p_scores, 1)

            def turn_probs(n):
                i, g, kind, r, k0, nk = units[n]
                src = ST[:, 0:P] if kind == "cmp" else PB[:, n % 2, :]
                pe.wait_ge(p_exp, n + 1)
                if n >= 1:
                    pe.wait_ge(p_c0, n)
                for k in range(first[n]):
                    mm = pe.transpose(PS[:, 4, k * P:(k + 1) * P], src[:, k * P:(k + 1) * P], ident)
                mm.then_inc(p_t0, 1)
                if nk > first[n]:
                    if t1_upto[n]:
                        pe.wait_ge(p_c1, t1_upto[n])
                    for k in range(first[n], nk):
                        mm = pe.transpose(PS[:, 5, (k - first[n]) * P:(k - first[n] + 1) * P], src[:, k * P:(k + 1) * P], ident)
                    mm.then_inc(p_t1, 1)

            def values(n):
                i, g, kind, r, k0, nk = units[n]
                pe.wait_ge(p_c0, n + 1)
                if kind == "cmp":
                    if 2 * i + g:
                        pe.wait_ge(p_mixed, 2 * i + g)
                    mm = pe.matmul(PS[:, 6, 0:R * HD], PTB[:, n % 2, 0:P], VBD[:, g, :], start=True, stop=True)
                else:
                    out = PS[:, 6, (R + r) * HD:(R + r + 1) * HD] if kind == "win" else PS[:, 7, r * HD:(r + 1) * HD]
                    v = VNAT[:, 1 if kind == "win" else 0, :, :]
                    for k in range(nk):
                        if k == first[n]:
                            pe.wait_ge(p_c1, t1_upto[n + 1])
                        mm = pe.matmul(out, PTB[:, n % 2, k * P:(k + 1) * P], v[:, k0 + k, g * HD:(g + 1) * HD],
                                       start=(k == 0), stop=(k == nk - 1))
                mm.then_inc(p_pv, 1)

            def turn_out(i):
                pe.wait_ge(p_mixed, 2 * i + 2)
                if i:
                    pe.wait_ge(p_olo, i)
                if t1_at:
                    pe.wait_ge(p_c1, t1_at)
                for r in range(R):
                    mm = pe.transpose(PS[:, 5, r * P:(r + 1) * P], OC[:, r, :, :].rearrange("p g d -> p (g d)"), ident)
                mm.then_inc(p_ot, 1)

            pe.wait_ge(ln_x, NCH)
            scores(0)
            scores(1)
            for n, u in enumerate(units):
                if u[2] == "win" and u[1] == 0 and u[3] == 0 and u[0]:
                    t1_at = t1_upto[n]
                    turn_out(u[0] - 1)
                    pe.wait_ge(p_olo, u[0])
                turn_probs(n)
                if n + 2 < len(units):
                    scores(n + 2)
                values(n)
            t1_at = t1_upto[len(units)]
            turn_out(QT_N - 1)

            pe.wait_ge(p_olo, QT_N)
            pe.wait_ge(p_mixed, 2 * QT_N)
            project("out", AT_OUT, KT)

            def ffn(st, layer, n0):
                def hidden(n, s, bank_set, use):
                    pe.wait_ge(set_free[st][bank_set], use + 1)
                    tile(n, s, bank_set, st)

                def second(n, s, it):
                    pe.wait_ge(w_split, n + (2 + RING))
                    for q in range(2):
                        pe.wait_ge(hl_done[q], it + layer * FG)
                    for m in range(KT):
                        for c in range(NCH):
                            e = m * NCH + c
                            pe.wait_ge(y_free[e % 2], it * 12 + (e // 2 - 12 + 1 + 12 * FG * layer))
                            for q in range(2):
                                mm = passes(PS[:, 6 + e % 2, 0:CH], weight((s + q) % RING, m * P),
                                            (HH[:, q, c * CH:(c + 1) * CH], HL[:, q, c * CH:(c + 1) * CH]),
                                            q == 0, q == 1)
                            mm.then_inc(y_full[e % 2], 1)
                    used[0] += 2

                for q in range(4):
                    hidden(n0 + q, (n0 + q) % RING, q % 2, q // 2)
                with pe.Fori(1, FG) as it:
                    at = 6 * it - 2
                    for q in range(2):
                        hidden(at + (n0 + q), (n0 + 4 + q) % RING, q, it * 2)
                    second(at + (n0 + 2), (n0 + 6) % RING, it)
                    for q in range(2):
                        hidden(at + (n0 + 4 + q), (n0 + 8 + q) % RING, q, it * 2 + 1)
                second(n0 + N_FFN - 2, (n0 + N_FFN - 2) % RING, FG)

            layer_norm(1, Y, ones_d, KT, 3, None)
            pe.wait_ge(ln_x, 6)
            ffn("f0", 0, AT_F0)
            layer_norm(2, Y, ones_d, KT, 6, None)

            pe.wait_ge(ln_x, 9)
            project("inc", AT_INC, KT)
            for g in range(4):
                n = AT_GRP + g // 2
                pe.wait_ge(dl_done, 8)
                for m in range(2):
                    pe.wait_ge(free["grp"], 2 * g + m + 1)
                    tile(n, n % RING, m, "grp", col=(g % 2) * 512 + m * 256, ks=range(2 * g, 2 * g + 2),
                         release=(g % 2 == 1 and m == 1))
            pe.wait_ge(zl_done, 8)
            project("outc", AT_OUTC, KT)
            layer_norm(3, Y, ones_d, KT, 9, None)
            pe.wait_ge(ln_x, 12)
            ffn("f1", 1, AT_F1)
            layer_norm(4, Y, ones_d, KT, 12, None)

        @block.scalar
        def _(act):
            for s in free.values():
                act.sem_inc(s, 2)
            for s in set_free.values():
                act.sem_inc(s[0], 1)

            def banks(s):
                return PS[:, 3 * s:3 * s + 3, 0:CH]

            def chunks(ap):
                return ap.rearrange("p (c t) -> p c t", c=NCH)

            act.dma_start(PEC[:, :, :], pe_t).then_inc(pe_loaded, 16)
            for k in range(KT):
                act.wait_ge(x_loaded, 16 * KT)
                act.activation(XH[:, k, :], XRAW[:, k, :], ACT.Copy).then_inc(x_hi, 1)

            rots = sgs = 0
            act.wait_ge(hist_loaded, 16 * CT)
            for n, name in enumerate(IN_ORDER):
                src = banks(n % 2)
                act.wait_ge(full["in"], n + 1)
                if name in ("ks", "kw") or name[0] == "q":
                    dst = QT[:, int(name[1]), :] if name[0] == "q" else kv(name)
                    act.activation(chunks(dst), src, ACT.Copy).then_inc(rot_full, 1)
                    if rots:
                        act.wait_ge(rot_free, rots)
                    for q in range(4):
                        o = q ^ 1
                        ins = act.activation(chunks(ROT[32 * q:32 * q + 32, :]), src[32 * o:32 * o + 32], ACT.Copy)
                        ins.then_inc(rot_full, 1)
                    rots += 1
                    act.wait_ge(rot_full, 5 * rots)
                elif name[:2] == "gb":
                    if sgs:
                        act.wait_ge(sg_free, sgs)
                    sgs += 1
                    act.activation(chunks(SG[:, :]), src, ACT.Sigmoid).then_inc(sg_full, 1)
                    act.wait_ge(sg_full, sgs)
                elif name[:2] == "ga":
                    c = int(name[2])
                    act.activation(UE[:, c, CW - 1:CW - 1 + 2 * CH].rearrange("p (c t) -> p c t", c=2), src[:, 0:2, :], ACT.Copy).then_inc(ga_full, 1)
                    act.activation(UE[:, c, CW - 1 + 2 * CH:UEP], src[:, 2, 0:LAST], ACT.Copy).then_inc(ga_full, 1)
                    act.activation(UE[:, c, UEP:].rearrange("p (b u) -> p b u", b=SB)[:, :, CW - 1:],
                                   src[:, 2, LAST:LAST + SB * SS].rearrange("p (b s) -> p b s", b=SB), ACT.Copy).then_inc(ga_full, 1)
                    act.wait_ge(ga_full, 3 * (c + 1))
                elif name == "gl":
                    act.wait_ge(sg_free, CT)
                    act.activation(chunks(GT[0:24, :]), src[0:24], ACT.Sigmoid).then_inc(gl_done, 1)
                    act.wait_ge(gl_done, 1)
                else:
                    act.activation(chunks(kv(name)), src, ACT.Copy).then_inc(kv_evac, 1)
                    act.wait_ge(kv_evac, {"kc": 1, "vc": 2, "vs": 3, "vw": 4}[name])
                act.sem_inc(free["in"], 1)

            for n, (srcs, dst, rows) in enumerate(TURNS):
                act.wait_ge(turned, n + 1)
                if n == 0:
                    act.wait_ge(kv_stored, 11 * 16)
                    act.wait_ge(job_done, 4)
                act.activation(dst, PS[0:rows, 4 + n % 2, 0:4 * P].rearrange("p (j t) -> p j t", j=4), ACT.Copy).then_inc(turned_out, 1)
            act.wait_ge(turned, T_GATE + 1)
            act.activation(GN[:, :, :].rearrange("p i n -> p (i n)"), PS[:, 4 + T_GATE % 2, 0:QT_N * 24], ACT.Copy).then_inc(turned_out, 1)
            act.wait_ge(turned, T_VBD + 1)
            act.wait_ge(vbd_zero, 1)
            for g in range(G):
                for r in range(R):
                    ins = act.activation(VBD[32 * r:32 * r + 32, g, r * HD:(r + 1) * HD],
                                         PS[0:NB, 4 + T_VBD % 2, g * HD:(g + 1) * HD], ACT.Copy)
                    ins.then_inc(vbd_in, 1)
            act.wait_ge(vbd_in, G * R)
            act.sem_inc(turned_out, 1)

            turn = 0
            for gi in range(4):
                act.wait_ge(s_cexp_in, gi + 1)
                act.activation(ST[:, 32:64], ST[:, 0:32], ACT.Exp, scale=SCALE).then_inc(s_cexp, 1)

                def move(dsts):
                    nonlocal turn
                    act.wait_ge(s_turn, turn + 1)
                    for dst, src in dsts:
                        ins = act.activation(dst, src, ACT.Copy)
                    ins.then_inc(s_turned, 1)
                    turn += 1

                for kind in range(2):
                    act.wait_ge(s_masked, 2 * gi + kind + 1)
                    n = (W_HIST, 8 * P)[kind] + SS
                    act.activation(PB[:, kind, 0:n], PB[:, kind, 0:n], ACT.Exp, bias=ST[:, 200 + kind:201 + kind], scale=SCALE,
                                   accum_out=ST[:, 204 + kind:205 + kind]).then_inc(s_exp, 1)
                    if kind == 0:
                        if gi:
                            act.wait_ge(s_pv, 3 * gi)
                        move([(PTB[0:NB, 0, 0:P], PS[0:NB, 6, 0:P])])
                        act.wait_ge(s_pv, 3 * gi + 1)
                        move([(PTB[:, 0, 0:4 * P], PS[:, 6, 0:4 * P])])
                        move([(PTB[0:SS, 0, 4 * P:5 * P], PS[0:SS, 6, 0:P])])
                    else:
                        act.wait_ge(s_pv, 3 * gi + 2)
                        move([(PTB[:, 0, 0:4 * P], PS[:, 6, 0:4 * P])])
                        move([(PTB[:, 1, 0:4 * P], PS[:, 6, 0:4 * P])])
                        move([(PTB[0:SS, 0, 4 * P:5 * P], PS[0:SS, 6, 0:P])])

            def layer_norm(L, src, nk, base_n, split=True):
                sq, rs = (SQC, RSC) if nk == CT else (SQ, RS)
                for c in range(NCH):
                    act.wait_ge(ln_cent, base_n + c + 1)
                    if base_n + c and c:
                        act.wait_ge(ln_var, base_n + c)
                    act.activation(sq[:, 0:nk, :], src[:, :, c * CH:(c + 1) * CH], ACT.Square).then_inc(ln_sq, 1)
                for c in range(NCH):
                    act.wait_ge(ln_ve, base_n + c + 1)
                    act.activation(rs[:, :], rs[:, :], ACT.Sqrt).then_inc(ln_sqrt, 1)
                    if nk == CT:
                        act.wait_ge(ln_norm, base_n + c + 1)
                        act.activation(src[:, :, c * CH:(c + 1) * CH], src[:, :, c * CH:(c + 1) * CH], ACT.Silu).then_inc(cv_act, 1)
                        act.wait_ge(cv_act, c + 1)
                        act.activation(XH[:, 4:8, c * CH:(c + 1) * CH], src[:, :, c * CH:(c + 1) * CH], ACT.Copy).then_inc(ln_hi, 1)
                    elif split:
                        act.wait_ge(ln_norm, base_n + c + 1)
                        act.activation(XH[:, :, c * CH:(c + 1) * CH], src[:, :, c * CH:(c + 1) * CH], ACT.Copy).then_inc(ln_hi, 1)

            layer_norm(0, CA, CT, 0)
            act.wait_ge(s_ms, 4)
            act.activation(XH[:, 0:4, NP_TOK:T], MS[:, :, :], ACT.Copy).then_inc(ms_hi, 1)

            def exps(n):
                i, g, kind, r, k0, nk = units[n]
                if kind == "cmp":
                    act.wait_ge(p_cin, 2 * i + g + 1)
                    act.activation(ST[:, 0:P], ST[:, 0:P], ACT.Exp, scale=SCALE).then_inc(p_cexp, 1)
                    act.wait_ge(p_cexp, 2 * i + g + 1)
                    return
                act.wait_ge(p_masked, n + 1)
                at = 208 + 4 * (kind == "sel") + r
                act.activation(PB[:, n % 2, 0:nk * P], PB[:, n % 2, 0:nk * P], ACT.Exp, bias=ST[:, 220 + n % 2:221 + n % 2],
                               scale=SCALE, accum_out=ST[:, at:at + 1]).then_inc(p_exp, 1)

            def out_high(i):
                act.wait_ge(p_ot, i + 1)
                act.activation(XH[:, 0:4, i * P:(i + 1) * P], PS[:, 5, :].rearrange("p (r q) -> p r q", r=R), ACT.Copy).then_inc(p_ohi, 1)

            exps(0)
            for n, u in enumerate(units):
                if n + 1 < len(units):
                    exps(n + 1)
                if u[2] == "win" and u[1] == 0 and u[3] == 0 and u[0]:
                    out_high(u[0] - 1)
                if u[5] > first[n]:
                    act.wait_ge(p_t1, t1_upto[n + 1])
                    if n >= 2:
                        act.wait_ge(p_pv, n - 1)
                    act.activation(PTB[:, n % 2, first[n] * P:u[5] * P], PS[:, 5, 0:(u[5] - first[n]) * P], ACT.Copy).then_inc(p_c1, 1)
            out_high(QT_N - 1)

            def ffn(st):
                def pair(it, first_pair):
                    for q in range(2):
                        act.wait_ge(full[st], it * 4 + (2 * q + 1))
                        if q or not first_pair:
                            act.wait_ge(ht_done[1 - q], it * 1 + q + ht_base[0])
                        act.activation(chunks(SL[:, :]), banks(0), ACT.Silu).then_inc(silu_done[q], 1)
                        act.wait_ge(silu_done[q], it + (1 + ht_base[0]))
                        act.sem_inc(set_free[st][0], 1)
                        act.wait_ge(ht_done[q], it + (1 + ht_base[0]))
                        if not first_pair:
                            act.wait_ge(y_full[1], it * 12 + 12 * ht_base[0])
                        act.activation(HH[:, q, :], HT[:, q, :], ACT.Copy).then_inc(hh_done[q], 1)

                pair(0, True)
                with act.Fori(1, FG) as it:
                    pair(it, False)
                ht_base[0] += FG

            ht_base = [0]
            layer_norm(1, Y, KT, 3)
            ffn("f0")
            layer_norm(2, Y, KT, 6)

            act.wait_ge(ln_x, 9)
            for m in range(KT):
                act.dma_start(UP[:, m, PUP:].rearrange("p (b u) -> p b u", b=SB)[:, :, 0:PH],
                              hist_p[:, m]).then_inc(hp_loaded, 16)
            act.dma_start(INV[:, :, :], invc).then_inc(inv_loaded, 16)
            act.wait_ge(hp_loaded, 16 * KT)
            for m in range(KT):
                src = banks(m % 2)
                act.wait_ge(full["inc"], m + 1)
                act.activation(UP[:, m, PH:PH + 2 * CH].rearrange("p (c t) -> p c t", c=2), src[:, 0:2, :], ACT.Copy).then_inc(up_in, 1)
                act.activation(UP[:, m, PH + 2 * CH:PUP], src[:, 2, 0:LAST], ACT.Copy).then_inc(up_in, 1)
                act.activation(UP[:, m, PUP:].rearrange("p (b u) -> p b u", b=SB)[:, :, PH:],
                               src[:, 2, LAST:LAST + SB * SS].rearrange("p (b s) -> p b s", b=SB), ACT.Copy).then_inc(up_in, 1)
                act.wait_ge(up_in, 5 * m + 3)
                act.sem_inc(free["inc"], 1)
                act.activation(POUT[:, m, 0, :], UP[:, m, NP_TOK:PUP], ACT.Copy).then_inc(up_in, 1)
                act.activation(POUT[:, m, 1:, :], UP[:, m, PUP:].rearrange("p (b u) -> p b u", b=SB)[:, :, SS:], ACT.Copy).then_inc(up_in, 1)
            act.wait_ge(up_in, 5 * KT)
            act.dma_start(poolT, POUT[:, :, :, :]).then_inc(stored, 16)
            for m in range(KT):
                act.wait_ge(d_done, 2 * (m + 1))
                act.wait_ge(full["inc"], KT)
                act.activation(XH[:, m, 0:NP_TOK], UP[:, m, PH:PUP], ACT.Copy).then_inc(dh_done, 1)
                act.activation(XH[:, m, NP_TOK:T].rearrange("p (b s) -> p b s", b=SB),
                               UP[:, m, PUP:].rearrange("p (b u) -> p b u", b=SB)[:, :, PH:], ACT.Copy).then_inc(dh_done, 1)
            for m in range(KT):
                act.wait_ge(full["grp"], 2 * (m // 2) + 2)
                act.activation(chunks(XH[:, m, :]), banks(m % 2), ACT.Identity, scale=PR[:, PR_SC + m:PR_SC + m + 1]).then_inc(zh_done, 1)
            layer_norm(3, Y, KT, 9)
            ffn("f1")
            layer_norm(4, Y, KT, 12, split=False)
            for c in range(NCH):
                act.wait_ge(ln_norm, 12 + c + 1)
                act.dma_start(yT[:, :, c * CH:(c + 1) * CH], Y[:, :, c * CH:(c + 1) * CH]).then_inc(stored, 16)
            act.wait_ge(stored, 16 * (1 + 1 + NCH))
            act.wait_ge(kv_stored, 11 * 16)

        @block.vector
        def _(dve):
            chain = [0]

            def link(ins):
                chain[0] += 1
                ins.then_inc(dv, 1)
                dve.wait_ge(dv, chain[0])

            def banks(s):
                return PS[:, 3 * s:3 * s + 3, 0:CH]

            def chunks(ap):
                return ap.rearrange("p (c t) -> p c t", c=NCH)

            for s in set_free.values():
                dve.sem_inc(s[1], 1)
            dve.memset(UE[:, :, 0:CW - 1], 0.0).then_inc(ue_zeroed, 1)
            for k in range(KT):
                dve.wait_ge(x_hi, k + 1)
                dve.tensor_tensor(XL[:, k, :], XRAW[:, k, :], XHf[:, k, :], ALU.subtract).then_inc(x_split, 1)
            dve.wait_ge(c_loaded, 5 * 16)

            rots = [0]

            def rope(dst):
                rots[0] += 1
                dve.wait_ge(rot_full, 5 * rots[0])
                dve.tensor_tensor(dst, dst, COS[:, :], ALU.mult).then_inc(dv, 1)
                dve.tensor_tensor(ROT[:, :], ROT[:, :], SIN[:, :], ALU.mult).then_inc(dv, 1)
                chain[0] += 2
                dve.wait_ge(dv, chain[0])
                dve.tensor_tensor(dst, dst, ROT[:, :], ALU.add).then_inc(roped, 1)
                dve.wait_ge(roped, rots[0])
                dve.sem_inc(rot_free, 1)

            def gate(c):
                dve.wait_ge(sg_full, c + 1)
                dve.wait_ge(ga_full, 3 * (c + 1))
                dve.tensor_tensor(UE[:, c, CW - 1:UEP], UE[:, c, CW - 1:UEP], SG[:, 0:NP_TOK], ALU.mult).then_inc(dv, 1)
                s = UE[:, c, UEP:].rearrange("p (b u) -> p b u", b=SB)[:, :, CW - 1:]
                dve.tensor_tensor(s, s, SG[:, NP_TOK:T].rearrange("p (b s) -> p b s", b=SB), ALU.mult).then_inc(dv, 1)
                chain[0] += 2
                dve.wait_ge(dv, chain[0])
                dve.sem_inc(sg_free, 1)
                dve.sem_inc(gated, 1)

            def conv(c, taps):
                for j in taps:
                    w = PR[:, PR_CW + c * CW + j:PR_CW + c * CW + j + 1]
                    parts = [(CA[:, c, 0:NP_TOK], UE[:, c, j:j + NP_TOK]),
                             (CA[:, c, NP_TOK:T].rearrange("p (b s) -> p b s", b=SB),
                              UE[:, c, UEP:].rearrange("p (b u) -> p b u", b=SB)[:, :, j:j + SS])]
                    for q, (dst, src) in enumerate(parts):
                        if j == 0:
                            dve.tensor_scalar(dst, src, w, PR[:, PR_CB + c:PR_CB + c + 1], ALU.mult, ALU.add).then_inc(conv_step, 1)
                        else:
                            dve.wait_ge(conv_step, 2 * (c * CW + j) + q - 1)
                            dve.scalar_tensor_tensor(out=dst, in0=src, scalar=w, in1=dst, op0=ALU.mult, op1=ALU.add).then_inc(conv_step, 1)

            dve.memset(CA[:, :, T:TP], 0.0).then_inc(ue_zeroed, 1)
            dve.wait_ge(ue_zeroed, 2)
            dve.wait_ge(hist_loaded, 16 * CT)
            rope(kv("ks"))
            rope(kv("kw"))
            gate(0)
            conv(0, range(CW))
            gate(1)
            conv(1, range(CW))
            gate(2)
            conv(2, range(0, 12))
            rope(QT[:, 0, :])
            conv(2, range(12, 20))
            rope(QT[:, 1, :])
            conv(2, range(20, CW))
            gate(3)
            rope(QT[:, 2, :])
            conv(3, range(0, 8))
            rope(QT[:, 3, :])
            conv(3, range(8, CW))

            dve.wait_ge(conv_step, 2 * CW * CT)
            dve.wait_ge(job_done, 4)
            dve.wait_ge(kv_stored, 11 * 16)
            dve.wait_ge(smp_c_loaded, 16)
            dve.wait_ge(att_c_loaded, 16)
            dve.memset(VBD[:, :, :], 0.0).then_inc(vbd_zero, 1)
            link(dve.tensor_copy(QS[:, :, :, :].rearrange("p b r s -> p r b s"),
                                 QT[:, :, NP_TOK:T].rearrange("p r (b s) -> p r b s", b=SB)))
            nkc = NB * (1 + SB)
            for kind in range(2):
                link(dve.tensor_copy(ST[:, 250 + kind:251 + kind], PS[:, kind, nkc:nkc + 1]))
            for kind in range(2):
                link(dve.tensor_scalar(KR[:, kind, :], PS[:, kind, 0:nkc], ST[:, 250 + kind:251 + kind], None, ALU.add))
            dve.sem_inc(kr_done, 1)
            rotc = PB[:, 0, 0:nkc]
            for q in range(4):
                o = q ^ 1
                link(dve.tensor_copy(PB[32 * q:32 * q + 32, 0, 0:nkc], KR[32 * o:32 * o + 32, 0, :]))
            link(dve.tensor_tensor(KCT[:, :], KR[:, 0, :], SMC[:, SC_COS:SC_COS + nkc], ALU.mult))
            link(dve.tensor_tensor(rotc, rotc, SMC[:, SC_SIN:SC_SIN + nkc], ALU.mult))
            dve.tensor_tensor(KCT[:, :], KCT[:, :], rotc, ALU.add).then_inc(kct_done, 1)
            dve.wait_ge(kct_done, 1)
            dve.wait_ge(turned_out, N_TURNS)
            dve.wait_ge(g_in, 16 * 16)

            for gi in range(4):
                dve.wait_ge(s_cmp, gi + 1)
                if gi:
                    dve.wait_ge(s_pv, 3 * gi)
                sc = ST[:, 0:32]
                link(dve.tensor_reduce(ST[:, 190:191], PS[:, 5, 0:NB], AX.X, ALU.max))
                dve.tensor_scalar(sc, PS[:, 5, 0:NB], ST[:, 190:191], None, ALU.subtract).then_inc(s_cexp_in, 1)
                dve.wait_ge(s_cexp, gi + 1)
                link(dve.tensor_reduce(ST[:, 191:192], ST[:, 32:64], AX.X, ALU.add))
                link(dve.reciprocal(ST[:, 191:192], ST[:, 191:192]))
                dve.tensor_scalar(ST[:, 64:96], ST[:, 32:64], ST[:, 191:192], None, ALU.mult).then_inc(s_pc, 1)
                dve.wait_ge(s_win, gi + 1)
                if gi:
                    dve.wait_ge(s_turned, 6 * gi)

                def masked(kind, parts):
                    for n, (dst, src, mask) in enumerate(parts):
                        link(dve.tensor_tensor_reduce(dst, src, mask, 1.0, -3.0e38, ALU.add, ALU.max, ST[:, 192 + n:193 + n]))
                    link(dve.tensor_tensor(ST[:, 194:195], ST[:, 192:193], ST[:, 193:194], ALU.max))
                    dve.tensor_scalar(ST[:, 200 + kind:201 + kind], ST[:, 194:195], -SCALE, None, ALU.mult).then_inc(s_masked, 1)
                    dve.wait_ge(s_masked, 2 * gi + kind + 1)

                masked(0, [(PB[:, 0, 0:W_HIST], PS[:, 0, :], SMC[:, SC_WM:SC_WM + W_HIST]),
                           (PB[:, 0, W_HIST:W_HIST + SS], PS[:, 1, 0:SS], SMC[:, SC_WM + W_HIST:SC_WM + W_HIST + SS])])
                dve.wait_ge(s_imp, gi + 1)
                link(dve.memset(ST[:, 128:145], 0.0))
                link(dve.tensor_reduce(ST[:, 128:144], PS[:, 5, 64:64 + NB].rearrange("p (b t) -> p b t", t=2), AX.X, ALU.add))
                link(dve.tensor_tensor(ST[:, 128:145], ST[:, 128:145], SMC[:, SC_SB:SC_SB + 17], ALU.add))
                link(dve.max(ST[:, 150:158], ST[:, 128:145]))
                link(dve.match_replace(ST[:, 160:177], ST[:, 150:158], ST[:, 128:145], TAKEN))
                link(dve.tensor_scalar(ST[:, 160:176], ST[:, 160:176], TAKEN, -1.0, ALU.is_equal, ALU.add))
                link(dve.tensor_scalar(ST[:, 160:176], ST[:, 160:176], BIG, None, ALU.mult))
                dve.wait_ge(s_sel, gi + 1)
                masked(1, [(PB[:, 1, 0:8 * P].rearrange("p (b t) -> p b t", t=64),
                            PS[:, 2:4, :].rearrange("p a (b t) -> p (a b) t", t=64),
                            ST[:, 160:176, None].to_broadcast([P, 16, 64])),
                           (PB[:, 1, 8 * P:8 * P + SS], PS[:, 4, 0:SS], SMC[:, SC_NEW:SC_NEW + SS])])
                dve.wait_ge(s_exp, 2 * gi + 2)
                link(dve.reciprocal(ST[:, 204:206], ST[:, 204:206]))
                link(dve.tensor_tensor(ST[:, 204:206], ST[:, 204:206], GNS[:, gi, 2:0:-1], ALU.mult))
                dve.wait_ge(s_pv, 3 * gi + 3)
                o = OC[:, 0, 0, :]
                link(dve.tensor_scalar(o, PS[:, 7, 0:HD], GNS[:, gi, 0:1], None, ALU.mult))
                link(dve.scalar_tensor_tensor(out=o, in0=PS[:, 7, HD:2 * HD], scalar=ST[:, 204:205], in1=o, op0=ALU.mult, op1=ALU.add))
                dve.scalar_tensor_tensor(out=o, in0=PS[:, 7, 2 * HD:3 * HD], scalar=ST[:, 205:206], in1=o, op0=ALU.mult, op1=ALU.add).then_inc(s_mixed, 1)
                dve.wait_ge(s_outT, gi + 1)
                for g in range(G):
                    for bb in range(2):
                        at = (2 * gi + bb) * SS
                        src = PS[0:HD, 5, 128 + 32 * (2 * bb + g):128 + 32 * (2 * bb + g) + 32]
                        link(dve.tensor_copy(MS[g * HD:(g + 1) * HD, :, at:at + SS], src.rearrange("p (r s) -> p r s", r=R)))
                dve.sem_inc(s_ms, 1)

            def layer_norm(L, src, nk, base_n, pg, pb, split=True):
                sq, rs = (SQC, RSC) if nk == CT else (SQ, RS)
                for c in range(NCH):
                    x = src[:, :, c * CH:(c + 1) * CH]
                    dve.wait_ge(ln_mean, base_n + c + 1)
                    mean = PS[:, c:c + 1, 0:CH].to_broadcast([P, nk, CH])
                    dve.tensor_tensor(x, x, mean, ALU.subtract).then_inc(ln_cent, 1)
                for c in range(NCH):
                    x = src[:, :, c * CH:(c + 1) * CH]
                    dve.wait_ge(ln_var, base_n + c + 1)
                    dve.tensor_scalar(rs[:, :], PS[:, 3 + c, 0:CH], EPS, None, ALU.add).then_inc(ln_ve, 1)
                    dve.wait_ge(ln_sqrt, base_n + c + 1)
                    link(dve.reciprocal(rs[:, :], rs[:, :]))
                    dve.wait_ge(ln_cent, base_n + c + 1)
                    link(dve.tensor_tensor(x, x, rs[:, None, :].to_broadcast([P, nk, CH]), ALU.mult))
                    for k in range(nk):
                        ins = dve.tensor_scalar(x[:, k, :], x[:, k, :], PR[:, pg + k:pg + k + 1], PR[:, pb + k:pb + k + 1], ALU.mult, ALU.add)
                        ins.then_inc(dv, 1)
                    chain[0] += nk
                    dve.wait_ge(dv, chain[0])
                    dve.sem_inc(ln_norm, 1)
                    if split:
                        dve.wait_ge(ln_hi, base_n + c + 1)
                        k0 = 4 if nk == CT else 0
                        dve.tensor_tensor(XL[:, k0:, c * CH:(c + 1) * CH], x, XHf[:, k0:, c * CH:(c + 1) * CH], ALU.subtract).then_inc(ln_x, 1)

            dve.wait_ge(s_exp, 8)
            dve.sem_inc(ln_in, NCH)
            layer_norm(0, CA, CT, 0, PR_CG, PR_CN)
            dve.wait_ge(ms_hi, 1)
            link(dve.tensor_tensor(XL[:, 0:4, NP_TOK:T], MS[:, :, :], XHf[:, 0:4, NP_TOK:T], ALU.subtract))
            link(dve.memset(XH[:, 0:4, T:TP].bitcast(F32), 0.0))
            link(dve.memset(XL[:, 0:4, T:TP].bitcast(F32), 0.0))

            def mask(n):
                i, g, kind, r, k0, nk = units[n]
                b = 2 * (n % 2)
                dve.wait_ge(p_scores, n + 1)
                if kind == "cmp":
                    m = 2 * i + g
                    sc = ST[:, 0:P].rearrange("p (r n) -> p r n", r=R)
                    cma = ATC[:, AC_CMA + i * NB:AC_CMA + (i + 1) * NB]
                    cmm = ATC[:, AC_CMM + i * NB:AC_CMM + (i + 1) * NB]
                    if n:
                        dve.wait_ge(p_t0, n)
                    dve.tensor_tensor(sc, PS[:, b, 0:P].rearrange("p (r n) -> p r n", r=R),
                                      cma[:, None, :].to_broadcast([P, R, NB]), ALU.add).then_inc(p_masked, 1)
                    dve.wait_ge(p_masked, n + 1)
                    link(dve.tensor_reduce(ST[:, 128:132], sc, AX.X, ALU.max))
                    dve.tensor_tensor(sc, sc, ST[:, 128:132, None].to_broadcast([P, R, NB]), ALU.subtract).then_inc(p_cin, 1)
                    dve.wait_ge(p_cexp, m + 1)
                    link(dve.tensor_tensor(sc, sc, cmm[:, None, :].to_broadcast([P, R, NB]), ALU.mult))
                    link(dve.tensor_reduce(ST[:, 128:132], sc, AX.X, ALU.add))
                    link(dve.tensor_scalar(ST[:, 128:132], ST[:, 128:132], TINY, None, ALU.max))
                    link(dve.reciprocal(ST[:, 128:132], ST[:, 128:132]))
                    dve.tensor_tensor(sc, sc, ST[:, 128:132, None].to_broadcast([P, R, NB]), ALU.mult).then_inc(p_exp, 1)
                    dve.wait_ge(p_exp, n + 1)
                    link(dve.tensor_reduce(ST[:, 136:152], ST[:, 0:P].rearrange("p (r b t) -> p b r t", r=R, t=2), AX.XY, ALU.add))
                    link(dve.tensor_tensor(ST[:, 136:152], ST[:, 136:152], ATC[:, AC_SB + i * 16:AC_SB + (i + 1) * 16], ALU.add))
                    link(dve.max(ST[:, 152:160], ST[:, 136:152]))
                    link(dve.match_replace(ST[:, 160:176], ST[:, 152:160], ST[:, 136:152], TAKEN))
                    link(dve.tensor_scalar(ST[:, 160:176], ST[:, 160:176], TAKEN, -1.0, ALU.is_equal, ALU.add))
                    w = 2 * (i + 1)
                    link(dve.tensor_scalar(SMASK[:, 0:w * 64].rearrange("p (b t) -> p b t", t=64),
                                           ST[:, 160:160 + w, None].to_broadcast([P, w, 64]), BIG, None, ALU.mult))
                    d = SMASK[:, i * P:(i + 1) * P]
                    link(dve.tensor_tensor(d, d, ATC[:, AC_CAUS:AC_CAUS + P], ALU.add))
                    return
                if n >= 2:
                    dve.wait_ge(p_t0, n - 1)
                    if t1_upto[n - 1]:
                        dve.wait_ge(p_t1, t1_upto[n - 1])
                w = nk * P
                msk = SMASK[:, 0:w] if kind == "sel" else ATC[:, AC_WM + 640 - w:AC_WM + 640]
                parts = [(0, min(w, 512))] + ([(512, w)] if w > 512 else [])
                src = PS[:, b, 0:w] if w <= 512 else PS[:, b:b + 2, :].rearrange("p a t -> p (a t)")[:, 0:w]
                link(dve.tensor_tensor_reduce(PB[:, n % 2, 0:w], src, msk, 1.0, -3.0e38, ALU.add, ALU.max, ST[:, 230:231]))
                dve.tensor_scalar(ST[:, 220 + n % 2:221 + n % 2], ST[:, 230:231], -SCALE, None, ALU.mult).then_inc(p_masked, 1)
                dve.wait_ge(p_masked, n + 1)

            def mix(i, g):
                n = last_of[(i, g)]
                gates = GN[:, i, g * 12:(g + 1) * 12].rearrange("p (r b) -> p b r", b=3)
                dve.wait_ge(p_exp, n + 1)
                link(dve.reciprocal(ST[:, 240:248], ST[:, 208:216]))
                link(dve.tensor_tensor(ST[:, 240:244], ST[:, 240:244], gates[:, 2, :], ALU.mult))
                link(dve.tensor_tensor(ST[:, 244:248], ST[:, 244:248], gates[:, 1, :], ALU.mult))
                if i and g == 0:
                    dve.wait_ge(p_ot, i)
                dve.wait_ge(p_pv, n + 1)
                o = OC[:, :, g, :]
                t = OTMP[:, :].rearrange("p (r d) -> p r d", r=R)

                def branch(bank, col):
                    return PS[:, bank, col:col + R * HD].rearrange("p (r d) -> p r d", r=R)

                link(dve.tensor_tensor(o, branch(6, 0), gates[:, 0, :, None].to_broadcast([P, R, HD]), ALU.mult))
                link(dve.tensor_tensor(t, branch(6, R * HD), ST[:, 240:244, None].to_broadcast([P, R, HD]), ALU.mult))
                link(dve.tensor_tensor(o, o, t, ALU.add))
                link(dve.tensor_tensor(t, branch(7, 0), ST[:, 244:248, None].to_broadcast([P, R, HD]), ALU.mult))
                dve.tensor_tensor(o, o, t, ALU.add).then_inc(p_mixed, 1)
                dve.wait_ge(p_mixed, 2 * i + g + 1)

            def out_low(i):
                dve.wait_ge(p_ohi, i + 1)
                dve.tensor_tensor(XL[:, 0:4, i * P:(i + 1) * P], PS[:, 5, :].rearrange("p (r q) -> p r q", r=R),
                                  XHf[:, 0:4, i * P:(i + 1) * P], ALU.subtract).then_inc(p_olo, 1)

            mask(0)
            for n, u in enumerate(units):
                if n and u[2] == "cmp":
                    mix(*units[n - 1][:2])
                if n + 1 < len(units) and units[n + 1][2] != "cmp":
                    mask(n + 1)
                if u[2] == "win" and u[1] == 0 and u[3] == 0 and u[0]:
                    out_low(u[0] - 1)
                dve.wait_ge(p_t0, n + 1)
                if n >= 2:
                    dve.wait_ge(p_pv, n - 1)
                dve.tensor_copy(PTB[:, n % 2, 0:first[n] * P], PS[:, 4, 0:first[n] * P]).then_inc(p_c0, 1)
                if n + 1 < len(units) and units[n + 1][2] == "cmp":
                    mask(n + 1)
            mix(QT_N - 1, G - 1)
            out_low(QT_N - 1)

            def residual(st, ln):
                for m in range(KT):
                    dve.wait_ge(full[st], m + 1)
                    y = chunks(Y[:, m, :])
                    dve.scalar_tensor_tensor(out=y, in0=y, scalar=ALPHA, in1=banks(m % 2), op0=ALU.mult, op1=ALU.add).then_inc(dv, 1)
                    chain[0] += 1
                    dve.wait_ge(dv, chain[0])
                    dve.sem_inc(free[st], 1)
                dve.sem_inc(ln_in, NCH)

            pairs_done = [0]

            def ffn(st):
                def hidden(it, q):
                    dve.wait_ge(full[st], it * 4 + (2 * q + 2))
                    dve.wait_ge(silu_done[q], it + (1 + pairs_done[0]))
                    dve.tensor_tensor(chunks(HT[:, q, :]), chunks(SL[:, :]), banks(1), ALU.mult).then_inc(ht_done[q], 1)
                    dve.wait_ge(ht_done[q], it + (1 + pairs_done[0]))
                    dve.sem_inc(set_free[st][1], 1)

                def low(it, q):
                    dve.wait_ge(hh_done[q], it + (1 + pairs_done[0]))
                    dve.tensor_tensor(HL[:, q, :], HT[:, q, :], HHf[:, q, :], ALU.subtract).then_inc(hl_done[q], 1)

                def sums(it, first_time):
                    for m in range(KT):
                        for c in range(NCH):
                            e = m * NCH + c
                            y = Y[:, m, c * CH:(c + 1) * CH]
                            acc = PS[:, 6 + e % 2, 0:CH]
                            dve.wait_ge(y_full[e % 2], it * 12 + (e // 2 - 12 + 1 + 12 * pairs_done[0]))
                            if first_time:
                                ins = dve.scalar_tensor_tensor(out=y, in0=y, scalar=ALPHA, in1=acc, op0=ALU.mult, op1=ALU.add)
                            else:
                                ins = dve.tensor_tensor(y, y, acc, ALU.add)
                            ins.then_inc(y_free[e % 2], 1)

                def last_sums():
                    for q in range(2):
                        dve.wait_ge(y_free[q], 1 + 12 * (FG + pairs_done[0]))

                for q in range(2):
                    hidden(0, q)
                    low(0, q)

                def step(it, first_time):
                    hidden(it, 0)
                    sums(it, first_time)
                    low(it, 0)
                    hidden(it, 1)
                    low(it, 1)

                step(1, True)
                with dve.Fori(2, FG) as it:
                    dve.wait_ge(y_free[0], it * 12 + (1 - 12 + 12 * pairs_done[0]))
                    dve.wait_ge(y_free[1], it * 12 + (1 - 12 + 12 * pairs_done[0]))
                    step(it, False)
                for q in range(2):
                    dve.wait_ge(y_free[q], 1 + 12 * (FG - 1 + pairs_done[0]))
                sums(FG, False)
                last_sums()
                pairs_done[0] += FG
                dve.sem_inc(ln_in, NCH)

            for q in range(2):
                dve.sem_inc(y_free[q], 1)
            dve.wait_ge(x_again, 16 * KT)
            residual("out", 1)
            layer_norm(1, Y, KT, 3, PR_LN, PR_LN + 8)
            ffn("f0")
            layer_norm(2, Y, KT, 6, PR_LN + 16, PR_LN + 24)

            dve.memset(UP[:, :, 0:PH], 0.0).then_inc(up_zero, 1)
            dve.wait_ge(up_zero, 1)
            dve.wait_ge(hp_loaded, 16 * KT)
            dve.wait_ge(inv_loaded, 16)
            for m in range(KT):
                group = m // 2
                dve.wait_ge(up_in, 5 * m + 5)
                src, w = UP[:, m, :], 1
                for s in range(group + 1):
                    dst = SUM[:, s % 2, :]
                    lo = 2 * w - 1
                    link(dve.tensor_tensor(dst[:, lo:], src[:, lo:], src[:, lo - w:PUW - w], ALU.add))
                    src, w = dst, 2 * w
                link(dve.tensor_tensor(src[:, PH:PH + 16], src[:, PH:PH + 16], INV[:, group, :], ALU.mult))
                for lo, hi in ((PH, PUP), (PUP + PH, PUW)):
                    dve.scalar_tensor_tensor(out=UP[:, m, lo:hi], in0=src[:, lo:hi], scalar=1.0 / w, in1=UP[:, m, lo:hi],
                                             op0=ALU.mult, op1=ALU.subtract).then_inc(d_done, 1)
                dve.wait_ge(d_done, 2 * m + 2)
            for m in range(KT):
                dve.wait_ge(dh_done, 2 * m + 2)
                link(dve.tensor_tensor(XL[:, m, 0:NP_TOK], UP[:, m, PH:PUP], XHf[:, m, 0:NP_TOK], ALU.subtract))
                dve.tensor_tensor(XL[:, m, NP_TOK:T].rearrange("p (b s) -> p b s", b=SB),
                                  UP[:, m, PUP:].rearrange("p (b u) -> p b u", b=SB)[:, :, PH:],
                                  XHf[:, m, NP_TOK:T].rearrange("p (b s) -> p b s", b=SB), ALU.subtract).then_inc(dl_done, 1)
            for m in range(KT):
                dve.wait_ge(zh_done, m + 1)
                dve.scalar_tensor_tensor(out=chunks(XL[:, m, :]), in0=banks(m % 2), scalar=PR[:, PR_SC + m:PR_SC + m + 1],
                                         in1=chunks(XHf[:, m, :]), op0=ALU.mult, op1=ALU.subtract).then_inc(zl_done, 1)
                dve.wait_ge(zl_done, m + 1)
                dve.sem_inc(free["grp"], 1)
            residual("outc", 3)
            layer_norm(3, Y, KT, 9, PR_LN + 32, PR_LN + 40)
            ffn("f1")
            layer_norm(4, Y, KT, 12, PR_LN + 48, PR_LN + 56, split=False)


def constants():
    import numpy as np
    f = np.float32
    c = {}
    eye = np.eye(P, dtype=f)
    c["consts"] = np.stack([eye, np.full((P, P), 1.0 / D, f), np.full((P, P), 1.0 / (CT * P), f)], 1)
    inv = (f(10000.0) ** (-np.arange(HD // 2, dtype=f) / f(HD // 2))).astype(f)

    def tables(pos):
        ang = (pos.astype(f)[None, :] * inv[:, None]).astype(f)
        cos, sin = np.cos(ang).astype(f), np.sin(ang).astype(f)
        return np.concatenate([cos] * 4, 0), np.concatenate([-sin, sin, -sin, sin], 0)

    pos = np.concatenate([np.arange(NP_TOK), np.tile(NP_TOK + np.arange(SS), SB), np.zeros(TP - T, int)])
    c["cosT"], c["sinT"] = tables(pos)
    q = np.arange(P)
    k = np.arange(P)
    caus = np.where(k[None] <= q[:, None], 0, -BIG).astype(f)
    kw = np.arange(640)
    wm = np.where((kw[None] > q[:, None]) & (kw[None] <= 512 + q[:, None]), 0, -BIG).astype(f)
    cma, sb = np.zeros((P, QT_N, NB), f), np.zeros((P, QT_N, 16), f)
    blk = np.arange(16)
    for i in range(QT_N):
        t = i * P + q
        cma[:, i] = np.where(np.arange(NB)[None] * 32 + 31 <= t[:, None], 0, -BIG)
        cur = (t // 64)[:, None]
        forced = (blk[None] == 0) | (blk[None] == cur) | (blk[None] == cur - 1)
        sb[:, i] = np.where(blk[None] * 64 <= t[:, None], np.where(forced, 1.0e4, 0.0), -1.0e4)
    c["att_c"] = np.concatenate([caus, wm, cma.reshape(P, -1), (cma == 0).astype(f).reshape(P, -1),
                                 sb.reshape(P, -1)], 1)
    pair, tok = q // 32, q % SS
    same = ((pair[:, None] == pair[None]) & (tok[:, None] == tok[None])).astype(f)
    j = np.arange(W_HIST + SS)
    swm = np.where((j[None] > tok[:, None]) & (j[None] <= W_HIST + tok[:, None]), 0, -BIG).astype(f)
    new = np.where(np.arange(SS)[None] <= tok[:, None], 0, -BIG).astype(f)
    ssb = np.zeros((P, 17), f)
    ssb[:, [0, 15, 16]] = 1.0e4
    cc, cs = tables(np.tile(np.arange(NB) * 32 + 31, 1 + SB))
    c["smp_c"] = np.concatenate([same, swm, new, ssb, cc, cs, np.zeros((P, 3), f)], 1)
    iv = np.ones((P, 4, 16), f)
    for g, w in enumerate((2, 4, 8, 16)):
        iv[:, g] = (f(w) / np.minimum(np.arange(16) + 1, w).astype(f))[None]
    c["invc"] = iv
    return {n: np.ascontiguousarray(a, dtype=f) for n, a in c.items()}


def layouts(i):
    import numpy as np
    a = {}
    xs = np.concatenate([i["x_prompt"].reshape(NP_TOK, D), i["x_sample"].reshape(SB * SS, D),
                         np.zeros((TP - T, D), np.float32)], 0)
    a["xT"] = xs.T.reshape(KT, P, TP)
    w_in = i["w_in_a"][0]
    cols = {}
    for r in range(R):
        cols[f"q{r}"] = np.concatenate([np.arange(HD) + (g * R + r) * HD for g in range(G)])
    for n, name in enumerate(("kc", "vc", "ks", "vs", "kw", "vw")):
        cols[name] = 512 + n * P + np.arange(P)
    for c in range(CT):
        cols[f"ga{c}"] = 512 + 768 + 24 + c * P + np.arange(P)
        cols[f"gb{c}"] = 512 + 768 + 24 + 512 + c * P + np.arange(P)
    cols["gl"] = 512 + 768 + np.arange(24)

    def out_tiles(w):
        kk, n = w.shape
        return w.reshape(kk // P, P, n // P, P).transpose(2, 1, 0, 3).reshape(n // P, P, kk)

    def in_tile(name):
        w = w_in[:, cols[name]]
        if w.shape[1] < P:
            w = np.concatenate([w, np.zeros((D, P - w.shape[1]), w.dtype)], 1)
        return out_tiles(w)[0]

    def ffn_tiles(l):
        w1, w3 = out_tiles(i["w1"][l]), out_tiles(i["w3"][l])
        w2 = i["w2"][l].reshape(FT, P, D)
        t = [w1[0], w3[0], w1[1], w3[1]]
        for g in range(1, FG):
            t += [w1[2 * g], w3[2 * g], w2[2 * g - 2], w2[2 * g - 1], w1[2 * g + 1], w3[2 * g + 1]]
        return t + [w2[FT - 2], w2[FT - 1]]

    wo = i["w_out_a"][0]
    rows = np.concatenate([cols[f"q{r}"] for r in range(R)] + [np.arange(512, 1024)])
    grp = i["w_grp_c"][0].reshape(2, 2, 2, P, 2, P)
    grp = grp.transpose(0, 3, 1, 4, 2, 5).reshape(2, P, 1024)
    a["wst"] = np.stack([in_tile(n) for n in IN_ORDER] + list(out_tiles(wo[rows])) + ffn_tiles(0)
                        + list(out_tiles(i["w_in_c"][0])) + list(grp) + list(out_tiles(i["w_out_c"][0])) + ffn_tiles(1))

    def per_feature(v):
        return v.reshape(-1, P).T

    cw = i["conv_w"][0].reshape(CW, CT, P).transpose(2, 1, 0).reshape(P, CT * CW)
    pr = [cw] + [per_feature(i[n][0]) for n in ("conv_b", "conv_ln_g", "conv_ln_b", "scale_c")]
    for l in range(2):
        pr += [per_feature(i[n][l]) for n in ("ln1_g", "ln1_b", "ln2_g", "ln2_b")]
    a["params"] = np.concatenate(pr, 1)
    a["pe_t"] = np.stack([np.concatenate([i[n][0].T] * 2, 0) for n in ("pe_cmp_k", "pe_cmp_v")], 1)
    for name, n in (("cw_k", "w_cmp_k"), ("cw_v", "w_cmp_v")):
        w = np.zeros((P, NB, P), np.float32)
        w[:HD, :, :HD] = w[HD:, :, HD:] = i[n][0].transpose(1, 0, 2)
        a[name] = w
    a["hist_c"] = i["state_conv"][0].reshape(SB, CW - 1, CT, P).transpose(3, 2, 0, 1)
    a["hist_p"] = i["state_pool"][0].reshape(SB, PH, KT, P).transpose(3, 2, 0, 1)
    c = i["cache_kv"][0].reshape(NPOOL, P, 4, P)
    a["cache"] = np.concatenate([c[:, :, 0:3].transpose(0, 3, 2, 1), c[:, :, 3:4]], 2)
    sw = i["state_win"][0].reshape(SB, W_HIST, 2, P)
    a["swk"] = sw[:, :, 0].transpose(0, 2, 1)
    a["swv"] = sw[:, :, 1].reshape(SB, 4, P, P).transpose(0, 2, 1, 3)
    a["win_past"] = sw[:, SS:]
    a["ptab"] = i["page_table"].reshape(1, SB * PAGES)
    return {n: np.ascontiguousarray(v) for n, v in a.items()}


_INS = ["xT", "wst", "params", "consts", "att_c", "smp_c", "cosT", "sinT", "pe_t", "cw_k", "cw_v", "hist_c", "hist_p",
        "invc", "cache", "swk", "swv", "win_past", "ptab"]
_OUTS = [("yT", (P, KT, TP)), ("kvT", (6, P, TP)), ("win_old", (SB, W_HIST - SS, 2, P)), ("convT", (P, CT, 9, CW - 1)),
         ("poolT", (P, KT, 9, PH))]


def results(o):
    import numpy as np
    y = o["yT"].transpose(2, 1, 0).reshape(TP, D)
    kvT, conv, pool = o["kvT"], o["convT"], o["poolT"]
    kv = kvT[:4].transpose(2, 0, 1).reshape(TP, 4, G, HD)
    win = kvT[4:].transpose(2, 0, 1).reshape(TP, 2, G, HD)
    new = win[NP_TOK:T].reshape(1, SB, SS, 2, G, HD)
    old = o["win_old"].reshape(1, SB, W_HIST - SS, 2, G, HD)
    conv = conv.transpose(2, 3, 1, 0).reshape(9, CW - 1, CT * P)
    pool = pool.transpose(2, 3, 1, 0).reshape(9, PH, D)
    return (y[None, :NP_TOK], y[NP_TOK:T].reshape(SB, SS, D), kv[None, None, :NP_TOK],
            kv[NP_TOK:T].reshape(1, SB, SS, 4, G, HD), win[None, None, NP_TOK - W_HIST:NP_TOK],
            np.concatenate([old, new], 2), conv[None, :1], conv[None, 1:], pool[None, :1], pool[None, 1:])


def kernel(**inputs):
    import numpy as _np
    import concourse.bacc as _bacc
    from concourse.bass_utils import run_bass_kernel_spmd as _run

    arrays = layouts({k: _np.asarray(v) for k, v in inputs.items()})
    arrays.update(constants())
    nc = _bacc.Bacc("TRN2", target_bir_lowering=False, num_devices=1)
    args = [nc.dram_tensor(n, arrays[n].shape, mybir.dt.from_np(arrays[n].dtype), kind="ExternalInput").ap()
            for n in _INS]
    args += [nc.dram_tensor(n, shape, F32, kind="ExternalOutput").ap() for n, shape in _OUTS]
    build(nc, *args)
    r = _run(nc, [arrays], core_ids=[0])
    return tuple(_np.ascontiguousarray(x) for x in results(r.results[0]))
```

```python
from contextlib import ExitStack

import concourse.bass as bass
from concourse import mybir

F32 = mybir.dt.float32
F32R = mybir.dt.float32r
I32 = mybir.dt.int32
ACT = mybir.ActivationFunctionType
ALU = mybir.AluOpType
AX = mybir.AxisListType

P = 128
D = 1024
KT = D // P
NP_TOK = 1024
SB, SS = 8, 8
T = NP_TOK + SB * SS
CH = 364
NCH = 3
TP = CH * NCH
LAST = NP_TOK - 2 * CH
HD, G, R = 64, 2, 4
QT_N = NP_TOK // P
CW = 31
CT = 4
UEP = CW - 1 + NP_TOK
UES = CW - 1 + SS
UEW = UEP + SB * UES
FT = 22
FG = FT // 2
NB = 32
PAGES = 8
JOB = 32
BATCH = 8
NPOOL = 80
BIG = 1.0e30
TINY = 1.0e-30
EPS = 1e-5
SCALE = HD ** -0.5
ALPHA = 4 ** 0.25
TAKEN = -3.0e38
W_HIST = 512
PH = 15
PUP = PH + NP_TOK
PUS = PH + SS
PUW = PUP + SB * PUS

IN_ORDER = ["ks", "kw", "gb0", "ga0", "kc", "vc", "vs", "gb1", "ga1", "vw", "gb2", "ga2",
            "q0", "q1", "gb3", "ga3", "q2", "q3", "gl"]
KV_AT = {"kc": 0, "vc": 1, "ks": 2, "vs": 3, "kw": 4, "vw": 5}
N_IN = len(IN_ORDER)
N_FFN = 3 * FT
AT_IN, AT_OUT = 0, N_IN
AT_F0 = AT_OUT + KT
AT_INC = AT_F0 + N_FFN
AT_GRP = AT_INC + KT
AT_OUTC = AT_GRP + 2
AT_F1 = AT_OUTC + KT
N_W = AT_F1 + N_FFN
POOL_ORDER = [6, 7, 4, 5, 2, 3, 0, 1]
RING = 3
WARM_START, WARM_GROUP = 6, 2
CONV_STEPS = 3
EARLY = 24
assert N_W % RING == 0 and EARLY % RING == 0

PR_CW, PR_CB, PR_CG, PR_CN = 0, CT * CW, CT * CW + 4, CT * CW + 8
PR_SC = PR_CN + 4
PR_LN = PR_SC + 8
PR_N = PR_LN + 64
AC_CAUS, AC_WM = 0, P
AC_CMA = AC_WM + 640
AC_CMM = AC_CMA + QT_N * NB
AC_SB = AC_CMM + QT_N * NB
AC_N = AC_SB + QT_N * 16
SC_G, SC_WM = 0, P
SC_NEW = SC_WM + W_HIST + SS
SC_SB = SC_NEW + SS
SC_COS = SC_SB + 17
SC_SIN = SC_COS + NB * (1 + SB)
SC_N = SC_SIN + NB * (1 + SB) + 3


def build(nc, xT, wst, params, consts, att_c, smp_c, cosT, sinT, pe_t, cw_k, cw_v, hist_c, hist_p, invc,
          cache, swk, swv, win_past, ptab, yT, kvT, win_old, convT, poolT):
    ctx = ExitStack()
    base = [16512]

    def place(name, shape, dt, at):
        return nc.alloc_sbuf_tensor_at(name, shape, dt, offset=at)

    def size(*dims):
        n = 4
        for d in dims:
            n *= d
        return -(-n // 32) * 32

    def region(n):
        at = base[0]
        base[0] += n
        return at

    r_x = region(2 * size(KT, TP))
    r_y = region(size(KT, TP))
    r_w = region(3 * size(RING, 1024))
    r_c = region(size(3 * P) + size(PR_N))
    r_f = base[0]
    end = nc.sbuf_usable_end

    XH = place("XH", [P, KT, TP], F32R, r_x)
    XL = place("XL", [P, KT, TP], F32R, r_x + size(KT, TP))
    XHf, XLf = XH[:, :, :].bitcast(F32), XL[:, :, :].bitcast(F32)
    Y = place("Y", [P, KT, TP], F32, r_y)
    XRAW = place("XRAW", [P, KT, TP], F32, r_y)
    RAW = place("RAW", [P, RING, 1024], F32, r_w)
    WH = place("WH", [P, RING, 1024], F32R, r_w + size(RING, 1024))
    WL = place("WL", [P, RING, 1024], F32R, r_w + 2 * size(RING, 1024))
    CST = place("CST", [P, 3, P], F32, r_c)
    PR = place("PR", [P, PR_N], F32, r_c + size(3 * P))
    ident, ones_d, ones_c = CST[:, 0, :], CST[:, 1, :], CST[:, 2, :]

    QT = place("QT", [P, R, TP], F32, r_y)
    KV4 = place("KV4", [P, 4, TP], F32, r_y + size(R, TP))
    KV2 = place("KV2", [P, 2, TP], F32, r_f)
    CA = place("CA", [P, CT, TP], F32, r_f + size(2, TP))
    r_u = r_f + size(2, TP) + size(CT, TP)
    UE = place("UE", [P, CT, UEW], F32, r_u)
    r_t = r_u + size(CT, UEW)
    COS = place("COS", [P, TP], F32, r_t)
    SIN = place("SIN", [P, TP], F32, r_t + size(TP))
    ROT = place("ROT", [P, TP], F32, r_t + 2 * size(TP))
    SG = place("SG", [P, TP], F32, r_t + 3 * size(TP))
    GT = place("GT", [24, TP], F32, r_t + 3 * size(TP))
    PTAB = place("PTAB", [1, 64], I32, r_t + 4 * size(TP))
    GN = place("GN", [P, QT_N, 24], F32, r_t + 4 * size(TP) + 256)
    GNS = place("GNS", [P, 4, 3], F32, r_t + 4 * size(TP) + 256 + size(QT_N * 24))
    MS = place("MS", [P, R, SB * SS], F32, r_t + 4 * size(TP) + 256 + size(QT_N * 24) + 64)
    assert size(P) + r_t + 4 * size(TP) + 256 + size(QT_N * 24) + 64 + 1024 <= end

    def kv(name):
        i = KV_AT[name]
        return KV4[:, i, :] if i < 4 else KV2[:, i - 4, :]

    PG = place("PG", [P, 2, JOB, P], F32, r_x)
    CWK = place("CWK", [P, 32, P], F32, r_x + size(64, P))
    CWV = place("CWV", [P, 32, P], F32, r_x + size(96, P))
    g_bytes = size(16, 256) + size(2, 512) + size(2, 512)
    KVP = [place(f"KVP{i}", [P, 16, 2, P], F32, r_x + i * g_bytes) for i in range(2)]
    KWS = [place(f"KWS{i}", [P, 2, W_HIST], F32, r_x + i * g_bytes + size(16, 256)) for i in range(2)]
    VWS = [place(f"VWS{i}", [P, 2, 4, P], F32, r_x + i * g_bytes + size(16, 256) + size(2, 512)) for i in range(2)]
    VN = place("VN", [SS, 2, SB, P], F32, r_x + 2 * g_bytes)
    VCS = place("VCS", [NB, SB, P], F32, r_x + 2 * g_bytes + size(16, P))
    SMC = place("SMC", [P, SC_N], F32, r_x + 2 * g_bytes + size(24, P))
    assert 2 * g_bytes + size(24, P) + size(SC_N) <= 2 * size(KT, TP)
    VNAT = place("VNAT", [P, 2, QT_N, P], F32, r_y + size(R, TP))
    r_xh, r_xl = r_x + size(4, TP), r_x + size(KT, TP) + size(4, TP)
    QH = place("QH", [P, R, TP], F32R, r_xh)
    QL = place("QL", [P, R, TP], F32R, r_y)
    KH2 = place("KH2", [P, 2, TP], F32R, r_xl)
    KH = [KH2[:, i, :] for i in range(2)]
    KL = [place("KL0", [P, TP], F32R, r_y + size(R, TP) + size(2, TP)), place("KL1", [P, TP], F32R, r_f)]
    KCH = place("KCH", [P, NB], F32R, r_xl + size(2, TP))
    KCL = place("KCL", [P, NB], F32R, r_xl + size(2, TP) + size(NB))
    a = [r_u]

    def scratch(name, shape, dt=F32):
        t = place(name, shape, dt, a[0])
        a[0] += size(*shape[1:])
        return t

    ATC = scratch("ATC", [P, AC_N])
    KCT = scratch("KCT", [P, NB * (1 + SB)])
    VBD = scratch("VBD", [P, G, R * HD])
    QS = scratch("QS", [P, SB, R, SS])
    pb_at = a[0]
    PB = scratch("PB", [P, 2, 1056])
    PTB = scratch("PTB", [P, 2, 8 * P])
    PTC = place("PTC", [P, P], F32, r_t + 4 * size(TP) + 256 + size(QT_N * 24) + 64 + 1024)
    SMASK = scratch("SMASK", [P, 1024])
    OC = scratch("OC", [P, R, G, HD])
    OTMP = scratch("OTMP", [P, R * HD])
    ST = scratch("ST", [P, 288])
    assert a[0] <= r_t + 3 * size(TP), (a[0], r_t)
    KR = place("KR", [P, 2, NB * (1 + SB)], F32, a[0] - size(288) - size(256) - size(512) - size(1024))

    f = [r_f]

    def ffn_t(name, shape, dt=F32):
        t = place(name, shape, dt, f[0])
        f[0] += size(*shape[1:])
        return t

    HH = ffn_t("HH", [P, 2, TP], F32R)
    HL = ffn_t("HL", [P, 2, TP], F32R)
    HHf = HH[:, :, :].bitcast(F32)
    SL = ffn_t("SL", [P, TP])
    HT = ffn_t("HT", [P, 2, TP])
    SQ = ffn_t("SQ", [P, KT, CH])
    RS = ffn_t("RS", [P, 2, CH])
    assert f[0] <= end
    UP = place("UP", [P, KT, PUW], F32, r_f)
    s_at = r_f + size(KT, PUW)
    SUM = place("SUM", [P, 2, PUW], F32, s_at)
    POUT = place("POUT", [P, KT, 9, PH], F32, s_at + size(2, PUW))
    INV = place("INV", [P, 4, 16], F32, s_at + size(2, PUW) + size(KT, 9, PH))
    assert s_at + size(2, PUW) + size(KT, 9, PH) + 256 <= end
    SQC = place("SQC", [P, CT, CH], F32, pb_at)
    RSC = place("RSC", [P, NCH, CH], F32, r_t + 3 * size(TP))

    gsc = nc.dram_tensor("gate_bounce", (SB * SS, 24), F32, kind="Internal").ap()

    with ctx:
        PS = ctx.enter_context(nc.psum_tensor("PS", [P, 8, 512], F32))

        def sem(name):
            return ctx.enter_context(nc.semaphore(name))

        raw_loaded = [sem(f"raw_loaded{i}") for i in range(RING)]
        hi_done, pool_turn = sem("hi_done"), sem("pool_turn")
        w_split = sem("w_split")
        w_free = sem("w_free")
        c_loaded = sem("c_loaded")
        x_loaded = [sem(f"x_loaded{k}") for k in range(KT)]
        x_hi = sem("x_hi")
        x_split = sem("x_split")
        full = {s: sem(f"full_{s}") for s in ("in", "out", "f0", "inc", "grp", "outc", "f1")}
        free = {s: sem(f"free_{s}") for s in ("in", "out", "inc", "grp", "outc")}
        set_free = {s: [sem(f"set_free_{s}_{q}") for q in range(2)] for s in ("f0", "f1")}
        hist_loaded = sem("hist_loaded")
        ue_zeroed = sem("ue_zeroed")
        rot_full, rot_free = sem("rot_full"), sem("rot_free")
        sg_full, sg_free, ga_full = sem("sg_full"), sem("sg_free"), sem("ga_full")
        kv_evac = sem("kv_evac")
        roped = sem("roped")
        gated = sem("gated")
        conv_step = sem("conv_step")
        dv = sem("dv")
        gl_done = sem("gl_done")
        kv_stored, kc_stored = sem("kv_stored"), sem("kc_stored")
        cw_loaded = [sem("cw_loaded_k"), sem("cw_loaded_v")]
        pg_loaded = [sem("pg_loaded0"), sem("pg_loaded1")]
        pe_loaded, vbd_in = sem("pe_loaded"), sem("vbd_in")
        job_done = sem("job_done")
        cmp_acc = sem("cmp_acc")
        att_c_loaded = sem("att_c_loaded")
        smp_c_loaded = sem("smp_c_loaded")
        kr_done = sem("kr_done")
        turned, turned_out = sem("turned"), sem("turned_out")
        kct_done = sem("kct_done")
        vbd_zero = sem("vbd_zero")
        g_out, g_in = sem("g_out"), sem("g_in")
        sp_loaded = [sem("sp_loaded0"), sem("sp_loaded1")]
        s_cmp, s_win, s_sel = sem("s_cmp"), sem("s_win"), sem("s_sel")
        s_pc, s_imp = sem("s_pc"), sem("s_imp")
        s_cexp_in, s_cexp = sem("s_cexp_in"), sem("s_cexp")
        s_masked, s_exp = sem("s_masked"), sem("s_exp")
        s_turn, s_turned = sem("s_turn"), sem("s_turned")
        s_pv, s_mixed, s_outT, s_ms = sem("s_pv"), sem("s_mixed"), sem("s_outT"), sem("s_ms")
        ms_hi = sem("ms_hi")
        ln_in, ln_mean, ln_cent, ln_sq = sem("ln_in"), sem("ln_mean"), sem("ln_cent"), sem("ln_sq")
        ln_var, ln_ve, ln_sqrt, ln_norm, ln_hi, ln_x = (sem("ln_var"), sem("ln_ve"), sem("ln_sqrt"), sem("ln_norm"),
                                                 sem("ln_hi"), sem("ln_x"))
        cv_act = sem("cv_act")
        wn_scaled, wn_hi, wn_lo, wn_y = sem("wn_scaled"), sem("wn_hi"), sem("wn_lo"), sem("wn_y")
        p_scores, p_masked, p_exp = sem("p_scores"), sem("p_masked"), sem("p_exp")
        p_cin, p_cexp, p_cpc = sem("p_cin"), sem("p_cexp"), sem("p_cpc")
        q_hi, q_lo = sem("q_hi"), sem("q_lo")
        cv_hi, cv_lo = sem("cv_hi"), sem("cv_lo")
        p_t0, p_t1, p_c0, p_c1 = sem("p_t0"), sem("p_t1"), sem("p_c0"), sem("p_c1")
        p_pv, p_mixed = sem("p_pv"), sem("p_mixed")
        p_ot, p_ohi, p_olo = sem("p_ot"), sem("p_ohi"), sem("p_olo")
        silu_done = [sem("silu_done0"), sem("silu_done1")]
        ht_done = [sem("ht_done0"), sem("ht_done1")]
        hh_done = [sem("hh_done0"), sem("hh_done1")]
        hl_done = [sem("hl_done0"), sem("hl_done1")]
        y_full = [sem("y_full0"), sem("y_full1")]
        y_free = [sem("y_free0"), sem("y_free1")]
        x_again = sem("x_again")
        up_zero, up_in, d_done, dh_done, dl_done, zh_done, zl_done = (
            sem("up_zero"), sem("up_in"), sem("d_done"), sem("dh_done"), sem("dl_done"), sem("zh_done"), sem("zl_done"))
        hp_loaded = sem("hp_loaded")
        inv_loaded = sem("inv_loaded")
        stored = sem("stored")

        N_PROMPT_UNITS = []
        for i in range(QT_N):
            for g in range(G):
                N_PROMPT_UNITS.append((i, g, "cmp", 0, 0, 1))
                for r in range(R):
                    N_PROMPT_UNITS.append((i, g, "win", r, max(0, i - 4), min(i + 1, 5)))
                for r in range(R):
                    N_PROMPT_UNITS.append((i, g, "sel", r, 0, i + 1))
        units = N_PROMPT_UNITS
        first = [min(4, -(-u[5] // 2)) if u[5] > 1 else 1 for u in units]
        t1_upto = [0]
        for u, n in zip(units, first):
            t1_upto.append(t1_upto[-1] + (u[5] > n))
        big = [n for n, u in enumerate(units) if u[2] != "cmp"]
        big_upto = [0]
        for u in units:
            big_upto.append(big_upto[-1] + (u[2] != "cmp"))

        def buffer_read(n):
            return max(0, n - 3 if units[n - 2][2] == "cmp" else n - 1)

        last_of = {(u[0], u[1]): n for n, u in enumerate(units)}
        OUT_AT = 4
        GU = 1 + 2 * R
        SPLITS = [(QT[:, r, :], QH[:, r, :], QL[:, r, :]) for r in range(R)] + \
            [(kv("ks"), KH[0], KL[0][:, :]), (kv("kw"), KH[1], KL[1][:, :]),
             (KCT[:, 0:NB], KCH[:, :], KCL[:, :])]
        N_STORES = []
        block = ctx.enter_context(nc.Block())

        def turns():
            for k, name in enumerate(("vs", "vw")):
                for h in range(2):
                    yield [(kv(name)[:, (4 * h + j) * P:(4 * h + j + 1) * P], P, P) for j in range(4)], \
                        VNAT[:, k, 4 * h:4 * h + 4, :], P
            for k, name in enumerate(("vs", "vw")):
                for h in range(2):
                    yield [(kv(name)[:, NP_TOK + (4 * h + j) * SS:NP_TOK + (4 * h + j + 1) * SS], P, SS)
                           for j in range(4)], VN[:, k, 4 * h:4 * h + 4, :], SS
            for h in range(2):
                yield [(KR[:, 1, NB * (1 + 4 * h + j):NB * (2 + 4 * h + j)], P, NB) for j in range(4)], \
                    VCS[:, 4 * h:4 * h + 4, :], NB

        TURNS = list(turns())
        T_GATE, T_VBD = len(TURNS), len(TURNS) + 1
        N_TURNS = len(TURNS) + 2

        def page_loads(eng, job, part):
            n, b = JOB // 2, job % 2
            for i0 in range(0, n, BATCH):
                at = JOB * b + n * part + i0
                pages = [eng.value_load(PTAB[0:1, at + i:at + i + 1], min_val=0, max_val=NPOOL - 1) for i in range(BATCH)]
                if i0 == 0 and job == 0:
                    eng.wait_ge(full["in"], N_IN)
                    if part == 0:
                        eng.dma_start(CWK[:, :, :], cw_k).then_inc(cw_loaded[0], 16)
                        eng.dma_start(CWV[:, :, :], cw_v).then_inc(cw_loaded[1], 16)
                elif i0 == 0 and job >= 2:
                    eng.wait_ge(job_done, job - 1)
                for i, page in enumerate(pages):
                    eng.dma_start(PG[:, b, n * part + i0 + i, :], cache[bass.ds(page, 1), :, job // 2, :]
                                  .rearrange("a p n -> (a p) n")).then_inc(pg_loaded[b], 16)

        def sample_windows(eng, gi):
            b2 = gi % 2
            eng.dma_start(KWS[b2][:, :, :], swk[2 * gi:2 * gi + 2].rearrange("b p n -> p b n")).then_inc(sp_loaded[b2], 16)
            eng.dma_start(VWS[b2][:, :, :, :], swv[2 * gi:2 * gi + 2].rearrange("b p k n -> p b k n")).then_inc(sp_loaded[b2], 16)

        @block.sync
        def _(sp):
            sp.dma_start(CST[:, :, :], consts).then_inc(c_loaded, 16)
            sp.dma_start(PR[:, :], params).then_inc(c_loaded, 16)
            for k in range(KT):
                sp.dma_start(XRAW[:, k, :], xT[k]).then_inc(x_loaded[k], 16)
            sp.dma_start(COS[:, :], cosT).then_inc(c_loaded, 16)
            sp.dma_start(SIN[:, :], sinT).then_inc(c_loaded, 16)
            for c in range(CT):
                sp.dma_start(UE[:, c, UEP:].rearrange("p (b u) -> p b u", b=SB)[:, :, 0:CW - 1],
                             hist_c[:, c]).then_inc(hist_loaded, 16)
            sp.dma_start(PTAB[:, :], ptab).then_inc(c_loaded, 16)

            def weights(start, n, from_round=0):
                with sp.Fori(from_round, n // RING) as it:
                    for s in range(RING):
                        sp.wait_ge(w_split, it * RING + start + s + 1)
                        sp.dma_start(RAW[:, s, :], wst[bass.ds(it * RING + start + s, 1), :, :]
                                     .rearrange("a p n -> (a p) n")).then_inc(raw_loaded[s], 16)

            weights(0, EARLY, 1)
            sp.wait_ge(c_loaded, 5 * 16)
            for job in range(4):
                page_loads(sp, job, 0)
                if job == 0:
                    sp.wait_ge(gl_done, 1)
                    sp.wait_ge(roped, 6)
                    for n in range(2):
                        sp.dma_start(kvT[2 + n], KV4[:, 2 + n, :]).then_inc(kv_stored, 16)
                        sp.dma_start(kvT[4 + n], KV2[:, n, :]).then_inc(kv_stored, 16)
                    sp.dma_start(gsc.rearrange("t n -> n t"), GT[0:24, NP_TOK:T], allow_slow_non_contiguous=True).then_inc(g_out, 16)
            sp.wait_ge(gated, CT)
            sp.dma_start(convT[:, :, 0, :], UE[:, :, NP_TOK:UEP]).then_inc(kv_stored, 16)
            for c in range(CT):
                sp.dma_start(convT[:, c, 1:, :], UE[:, c, UEP:].rearrange("p (b u) -> p b u", b=SB)
                             [:, :, SS:]).then_inc(kv_stored, 16)
            sp.wait_ge(g_out, 16)
            rows = gsc.rearrange("(gi bb s) (g r br) -> g r bb s gi br", g=G, r=R, bb=2, s=SS)
            for bb in range(2):
                for g in range(G):
                    for r in range(R):
                        at = 32 * (2 * bb + g) + r * SS
                        sp.dma_start(GNS[at:at + SS, :, :], rows[g, r, bb]).then_inc(g_in, 16)
            sp.wait_ge(conv_step, 2 * CW * CT)
            sp.wait_ge(roped, 6)
            sp.wait_ge(kv_stored, 9 * 16)
            sp.dma_start(ATC[:, :], att_c).then_inc(att_c_loaded, 16)

            def sample_pages(gi):
                b2 = gi % 2
                for i0 in range(0, 2 * PAGES, BATCH):
                    at = 2 * PAGES * gi + i0
                    pages = [sp.value_load(PTAB[0:1, at + i:at + i + 1], min_val=0, max_val=NPOOL - 1) for i in range(BATCH)]
                    for i, page in enumerate(pages):
                        sp.dma_start(KVP[b2][:, i0 + i, :, :].rearrange("p k n -> p (k n)"),
                                     cache[bass.ds(page, 1), :, 2:4, :].rearrange("a p k n -> (a p) (k n)")
                                     ).then_inc(sp_loaded[b2], 16)

            sp.wait_ge(job_done, 3)
            sample_pages(0)
            sp.wait_ge(job_done, 4)
            for gi in range(1, 4):
                if gi >= 2:
                    sp.wait_ge(s_pv, 3 * (gi - 1))
                sample_pages(gi)
                sample_windows(sp, gi)
            sp.dma_start(win_old, win_past).then_inc(stored, 16)
            sp.wait_ge(p_pv, len(units))
            for k in range(KT):
                sp.dma_start(Y[:, k, :], xT[k]).then_inc(x_again, 16)
            weights(EARLY, N_W - EARLY)

        @block.gpsimd
        def _(pool):
            pool.sem_inc(w_split, RING)
            with pool.Fori(0, N_W // RING) as it:
                for s in range(RING):
                    pool.wait_ge(raw_loaded[s], it * 16 + 16)
                    pool.wait_ge(w_free, it * RING + s + 1)
                    pool.sem_inc(pool_turn, 1)
                    pool.tensor_copy(WH[:, s, :], RAW[:, s, :]).then_inc(hi_done, 1)
                    pool.wait_ge(hi_done, it * RING + s + 1)
                    pool.tensor_tensor(WL[:, s, :], RAW[:, s, :], WH[:, s, :].bitcast(F32),
                                       ALU.subtract).then_inc(w_split, 1)

        @block.tensor
        def _(pe):
            pe.sem_inc(w_free, RING)

            used = [0]

            def passes(out, w, x, start, stop):
                mm = pe.matmul(out, w[0], x[0], start=start, stop=False)
                if used[0]:
                    mm.then_inc(w_free, used[0])
                    used[0] = 0
                pe.matmul(out, w[1], x[0], start=False, stop=False)
                return pe.matmul(out, w[0], x[1], start=False, stop=stop)

            def weight(s, col):
                return WH[:, s, col:col + P], WL[:, s, col:col + P]

            def tile(n, s, bank_set, st, col=0, ks=range(KT), release=True, x_wait=False):
                pe.wait_ge(w_split, n + (1 + RING))
                for c in range(NCH):
                    for q, k in enumerate(ks):
                        if x_wait and c == 0:
                            pe.wait_ge(x_split, k + 1)
                        mm = passes(PS[:, 3 * bank_set + c, 0:CH], weight(s, col + q * P),
                                    (XH[:, k, c * CH:(c + 1) * CH], XL[:, k, c * CH:(c + 1) * CH]),
                                    q == 0, q == len(ks) - 1)
                mm.then_inc(full[st], 1)
                if release:
                    used[0] += 1

            def two_tiles(st, n0, L):
                pe.wait_ge(w_split, n0 + 2 + RING)
                for c in range(NCH):
                    pe.wait_ge(wn_lo, KT * (NCH * (L - 1) + c + 1))
                    for q in range(2):
                        for k in range(KT):
                            mm = passes(PS[:, 3 * q + c, 0:CH], weight((n0 + q) % RING, k * P),
                                        (XH[:, k, c * CH:(c + 1) * CH], XL[:, k, c * CH:(c + 1) * CH]), k == 0, k == KT - 1)
                        if c == NCH - 1:
                            mm.then_inc(full[st], 1)
                used[0] += 2

            def project(st, n0, count, after_norm=None):
                def one(n, s, q):
                    pe.wait_ge(free[st], n + 1)
                    tile(n0 + n, s, q % 2, st)

                if after_norm:
                    pe.wait_ge(free[st], 2)
                    two_tiles(st, n0, after_norm)
                    done = 2
                else:
                    pe.wait_ge(free[st], 1)
                    tile(n0, n0 % RING, 0, st, x_wait=(st == "in"))
                    done = 1
                loops = (count - done) // 6
                if loops > 1:
                    first_of = done
                    with pe.Fori(0, loops) as it:
                        for j in range(6):
                            one(it * 6 + (first_of + j), (n0 + first_of + j) % RING, first_of + j)
                    done += 6 * loops
                for n in range(done, count):
                    one(n, (n0 + n) % RING, n)

            def mean(src, ones, nk, b, c):
                pe.wait_ge(ln_in, b + c + 1)
                for k in range(nk):
                    mm = pe.matmul(PS[:, c, 0:CH], ones, src[:, k, c * CH:(c + 1) * CH], start=(k == 0), stop=(k == nk - 1))
                    if k == 0 and used[0]:
                        mm.then_inc(w_free, used[0])
                        used[0] = 0
                mm.then_inc(ln_mean, 1)

            def var(sq, ones, nk, b, c):
                pe.wait_ge(ln_sq, b + c + 1)
                for k in range(nk):
                    mm = pe.matmul(PS[:, 3 + c, 0:CH], ones, sq[:, k, :], start=(k == 0), stop=(k == nk - 1))
                mm.then_inc(ln_var, 1)

            def conv_norm():
                for c in range(NCH):
                    mean(CA, ones_c, CT, 0, c)
                for c in range(NCH):
                    var(SQC, ones_c, CT, 0, c)

            def wide_mean(L, c):
                mean(Y, ones_d, KT, NCH * L, c)

            def wide_var(L, c):
                var(SQ, ones_d, KT, NCH * L, c)

            def norm_start(L):
                wide_mean(L, 0)
                wide_mean(L, 1)
                wide_var(L, 0)

            def norm_rest(L):
                wide_mean(L, 2)
                wide_var(L, 1)
                wide_var(L, 2)

            def keep_warm(count, bank):
                for _ in range(count):
                    pe.matmul(PS[:, bank, 0:3 * P], ident, CST[:, :, :].rearrange("p a n -> p (a n)"), start=True, stop=True)

            project("in", AT_IN, N_IN)
            pe.wait_ge(c_loaded, 5 * 16)

            def compress(out, w, src):
                for p in range(NB):
                    mm = pe.matmul(out, w[:, p, :], src(p), start=(p == 0), stop=(p == NB - 1))
                return mm

            pe.wait_ge(free["in"], 2 + N_IN)
            pe.wait_ge(pe_loaded, 16 * 2)
            for kind, w in enumerate((CWK, CWV)):
                pe.wait_ge(cw_loaded[kind], 16)
                compress(PS[:, kind, 288:288 + NB + 1], w,
                         lambda p: KV4[:, kind, 0:NP_TOK + NB].rearrange("q (n p) -> q n p", p=NB)[:, :, p])
            for job in range(4):
                kind, half = job // 2, job % 2
                w = (CWK, CWV)[kind]
                pe.wait_ge(cw_loaded[kind], 16)
                pe.wait_ge(pg_loaded[half], JOB * 16 * (kind + 1))
                mm = compress(PS[:, kind, NB + half * P:NB + (half + 1) * P], w,
                              lambda p: PG[:, half, :, :].rearrange("q a (n p) -> q (a n) p", p=NB)[:, :, p])
                mm.then_inc(job_done, 1)

            def turn_bank(n):
                return 4 + n % 2

            pe.wait_ge(kr_done, 1)
            pe.wait_ge(roped, 6)
            for n, (srcs, _, rows) in enumerate(TURNS):
                if n >= 2:
                    pe.wait_ge(turned_out, n - 1)
                for j, (src, _, _) in enumerate(srcs):
                    mm = pe.transpose(PS[0:rows, turn_bank(n), j * P:(j + 1) * P], src, ident)
                mm.then_inc(turned, 1)
            pe.wait_ge(turned_out, T_GATE - 1)
            pe.wait_ge(gl_done, 1)
            for i in range(QT_N):
                mm = pe.transpose(PS[:, turn_bank(T_GATE), i * 24:(i + 1) * 24], GT[0:24, i * P:(i + 1) * P],
                                  ident[0:24, 0:24])
            mm.then_inc(turned, 1)
            pe.wait_ge(turned_out, T_VBD - 1)
            pe.transpose(PS[0:NB, turn_bank(T_VBD), 0:P], KR[:, 1, 0:NB], ident).then_inc(turned, 1)

            pe.wait_ge(turned_out, N_TURNS)
            pe.wait_ge(kct_done, 1)
            pe.wait_ge(smp_c_loaded, 16)
            turn = 0
            for gi in range(4):
                b2 = gi % 2

                def pairs():
                    for bb in range(2):
                        for g in range(G):
                            j = 2 * bb + g
                            at = NP_TOK + (2 * gi + bb) * SS
                            yield bb, g, slice(32 * j, 32 * j + 32), slice(g * HD, g * HD + HD), \
                                QS[g * HD:g * HD + HD, 2 * gi + bb, :, :].rearrange("p r s -> p (r s)"), at

                if gi:
                    pe.wait_ge(s_ms, gi)
                for bb, g, rows, feat, q, at in pairs():
                    mm = pe.matmul(PS[rows, 5, 0:NB], q, KCT[feat, NB * (1 + 2 * gi + bb):NB * (2 + 2 * gi + bb)],
                                   start=True, stop=True)
                mm.then_inc(s_cmp, 1)
                pe.wait_ge(sp_loaded[b2], 18 * 16 * (gi // 2 + 1))
                for bb, g, rows, feat, q, at in pairs():
                    pe.matmul(PS[rows, 0, :], q, KWS[b2][feat, bb, :], start=True, stop=True)
                    mm = pe.matmul(PS[rows, 1, 0:SS], q, kv("kw")[feat, at:at + SS], start=True, stop=True)
                mm.then_inc(s_win, 1)
                for bb, g, rows, feat, q, at in pairs():
                    for h in range(2):
                        pe.matmul(PS[rows, 2 + h, :], q, KVP[b2][feat, 8 * bb + 4 * h:8 * bb + 4 * h + 4, 0, :],
                                  start=True, stop=True)
                    mm = pe.matmul(PS[rows, 4, 0:SS], q, kv("ks")[feat, at:at + SS], start=True, stop=True)
                mm.then_inc(s_sel, 1)
                pe.wait_ge(s_pc, gi + 1)
                pe.matmul(PS[:, 5, 64:64 + NB], SMC[:, SC_G:SC_G + P], ST[:, 64:64 + NB], start=True, stop=True).then_inc(s_imp, 1)

                def turned_tiles(src, cols):
                    nonlocal turn
                    if turn:
                        pe.wait_ge(s_turned, turn)
                    for n, (lo, hi) in enumerate(cols):
                        mm = pe.transpose(PS[0:hi - lo, 6, n * P:(n + 1) * P], src[:, lo:hi], ident)
                    mm.then_inc(s_turn, 1)
                    turn += 1

                turned_tiles(ST, [(64, 64 + NB)])
                pe.wait_ge(s_turned, turn)
                for bb, g, rows, feat, q, at in pairs():
                    mm = pe.matmul(PS[rows, 7, 0:HD], PTB[0:NB, 0, rows], VCS[:, 2 * gi + bb, feat], start=True, stop=True)
                mm.then_inc(s_pv, 1)
                pe.wait_ge(s_exp, 2 * gi + 1)
                turned_tiles(PB[:, 0, :], [(k * P, k * P + P) for k in range(4)])
                turned_tiles(PB[:, 0, :], [(W_HIST, W_HIST + SS)])
                pe.wait_ge(s_turned, turn)
                for bb, g, rows, feat, q, at in pairs():
                    for k in range(4):
                        pe.matmul(PS[rows, 7, HD:2 * HD], PTB[:, 0, k * P + 32 * (2 * bb + g):k * P + 32 * (2 * bb + g) + 32],
                                  VWS[b2][:, bb, k, feat], start=(k == 0), stop=False)
                    mm = pe.matmul(PS[rows, 7, HD:2 * HD], PTB[0:SS, 0, 4 * P + 32 * (2 * bb + g):4 * P + 32 * (2 * bb + g) + 32],
                                   VN[:, 1, 2 * gi + bb, feat], start=False, stop=True)
                mm.then_inc(s_pv, 1)
                pe.wait_ge(s_exp, 2 * gi + 2)
                turned_tiles(PB[:, 1, :], [(k * P, k * P + P) for k in range(4)])
                turned_tiles(PB[:, 1, :], [(k * P, k * P + P) for k in range(4, 8)])
                turned_tiles(PB[:, 1, :], [(8 * P, 8 * P + SS)])
                pe.wait_ge(s_turned, turn)
                for bb, g, rows, feat, q, at in pairs():
                    j = 32 * (2 * bb + g)
                    for k in range(8):
                        pe.matmul(PS[rows, 7, 2 * HD:3 * HD], PTB[:, k // 4, (k % 4) * P + j:(k % 4) * P + j + 32],
                                  KVP[b2][:, 8 * bb + k, 1, feat], start=(k == 0), stop=False)
                    mm = pe.matmul(PS[rows, 7, 2 * HD:3 * HD], PTB[0:SS, 0, 4 * P + j:4 * P + j + 32],
                                   VN[:, 0, 2 * gi + bb, feat], start=False, stop=True)
                mm.then_inc(s_pv, 1)
                pe.wait_ge(s_mixed, gi + 1)
                pe.transpose(PS[0:HD, 5, 128:256], OC[:, 0, 0, :], ident).then_inc(s_outT, 1)

            pe.wait_ge(s_ms, 4)
            conv_norm()

            def product(out, w, x, start=True, stop=True):
                pe.matmul(out, w[0], x[0], start=start, stop=False)
                pe.matmul(out, w[1], x[0], start=False, stop=False)
                return pe.matmul(out, w[0], x[1], start=False, stop=stop)

            def scores(n):
                i, g, kind, r, k0, nk = units[n]
                b = 2 * (n % 2)
                feat = slice(g * HD, g * HD + HD)
                if n >= 2:
                    pe.wait_ge(p_masked, n - 1)
                if kind == "cmp":
                    for h in range(R):
                        q = [t[feat, h, i * P:(i + 1) * P] for t in (QH, QL)]
                        mm = product(PS[:, b, h * NB:(h + 1) * NB], q, [t[feat, :] for t in (KCH, KCL)])
                else:
                    q = [t[feat, r, i * P:(i + 1) * P] for t in (QH, QL)]
                    keys = [t[kind == "win"] for t in (KH, KL)]
                    for h in range(-(-nk // 4)):
                        w = min(4, nk - 4 * h) * P
                        at = (k0 + 4 * h) * P
                        mm = product(PS[:, b + h, 0:w], q, [t[feat, at:at + w] for t in keys])
                mm.then_inc(p_scores, 1)

            def turn_probs(n):
                i, g, kind, r, k0, nk = units[n]
                if n >= 1:
                    pe.wait_ge(p_c0, n)
                if kind == "cmp":
                    keep_warm(WARM_GROUP if n else WARM_START, 4 if n else 6)
                    src = ST[:, 0:P]
                    pe.wait_ge(p_cpc, n // GU + 1)
                else:
                    src = PB[:, n % 2, :]
                    pe.wait_ge(p_exp, big_upto[n + 1])
                for k in range(first[n]):
                    mm = pe.transpose(PS[:, 4, k * P:(k + 1) * P], src[:, k * P:(k + 1) * P], ident)
                mm.then_inc(p_t0, 1)
                if nk > first[n]:
                    if t1_upto[n]:
                        pe.wait_ge(p_c1, t1_upto[n])
                    if outs[0]:
                        pe.wait_ge(p_olo, outs[0])
                    for k in range(first[n], nk):
                        mm = pe.transpose(PS[:, 5, (k - first[n]) * P:(k - first[n] + 1) * P], src[:, k * P:(k + 1) * P], ident)
                    mm.then_inc(p_t1, 1)

            def values(n):
                i, g, kind, r, k0, nk = units[n]
                pe.wait_ge(p_c0, n + 1)
                if kind == "cmp":
                    if n // GU:
                        pe.wait_ge(p_mixed, n // GU)
                    mm = pe.matmul(PS[:, 6, 0:R * HD], PTC[:, :], VBD[:, g, :], start=True, stop=True)
                else:
                    out = PS[:, 6, (R + r) * HD:(R + r + 1) * HD] if kind == "win" else PS[:, 7, r * HD:(r + 1) * HD]
                    v = VNAT[:, 1 if kind == "win" else 0, :, :]
                    for k in range(nk):
                        if k == first[n]:
                            pe.wait_ge(p_c1, t1_upto[n + 1])
                        mm = pe.matmul(out, PTB[:, n % 2, k * P:(k + 1) * P], v[:, k0 + k, g * HD:(g + 1) * HD],
                                       start=(k == 0), stop=(k == nk - 1))
                mm.then_inc(p_pv, 1)

            outs = [0]

            def turn_out(i, n):
                pe.wait_ge(p_mixed, 2 * i + 2)
                if i:
                    pe.wait_ge(p_olo, i)
                if t1_upto[n]:
                    pe.wait_ge(p_c1, t1_upto[n])
                for r in range(R):
                    mm = pe.transpose(PS[:, 5, r * P:(r + 1) * P], OC[:, r, :, :].rearrange("p g d -> p (g d)"), ident)
                mm.then_inc(p_ot, 1)
                outs[0] += 1

            pe.wait_ge(q_lo, len(SPLITS))
            scores(0)
            scores(1)
            for n, u in enumerate(units):
                turn_probs(n)
                if n + 2 < len(units):
                    scores(n + 2)
                if u[0] and n % (2 * GU) == OUT_AT:
                    turn_out(u[0] - 1, n + 1)
                if n and units[n - 1][2] != "cmp":
                    if units[n - 2][2] == "cmp":
                        values(n - 2)
                    values(n - 1)
            values(len(units) - 1)
            turn_out(QT_N - 1, len(units))

            pe.wait_ge(p_olo, QT_N)
            pe.wait_ge(p_mixed, 2 * QT_N)
            pe.wait_ge(cv_lo, CT)
            project("out", AT_OUT, KT)

            def ffn(st, layer, n0):
                def hidden(n, s, bank_set, use):
                    pe.wait_ge(set_free[st][bank_set], use + 1)
                    tile(n, s, bank_set, st)

                def second(n, s, it, last=False):
                    pe.wait_ge(w_split, n + (2 + RING))
                    for q in range(2):
                        pe.wait_ge(hl_done[q], it + layer * FG)
                    order = [(m, c) for c in range(NCH) for m in range(KT)] if last else \
                        [(m, c) for m in range(KT) for c in range(NCH)]
                    for e, (m, c) in enumerate(order):
                        if last and e == KT + 2:
                            wide_mean(2 * layer + 2, 0)
                        if last and e == 2 * KT + 2:
                            wide_mean(2 * layer + 2, 1)
                            wide_var(2 * layer + 2, 0)
                        pe.wait_ge(y_free[e % 2], it * 12 + (e // 2 - 12 + 1 + 12 * FG * layer))
                        for q in range(2):
                            mm = passes(PS[:, 6 + e % 2, 0:CH], weight((s + q) % RING, m * P),
                                        (HH[:, q, c * CH:(c + 1) * CH], HL[:, q, c * CH:(c + 1) * CH]),
                                        q == 0, q == 1)
                        mm.then_inc(y_full[e % 2], 1)
                    used[0] += 2

                for q in range(2):
                    pe.wait_ge(set_free[st][q], 1)
                two_tiles(st, n0, 2 * layer + 1)
                for q in range(2, 4):
                    hidden(n0 + q, (n0 + q) % RING, q % 2, q // 2)
                with pe.Fori(1, FG) as it:
                    at = 6 * it - 2
                    for q in range(2):
                        hidden(at + (n0 + q), (n0 + 4 + q) % RING, q, it * 2)
                    second(at + (n0 + 2), (n0 + 6) % RING, it)
                    for q in range(2):
                        hidden(at + (n0 + 4 + q), (n0 + 8 + q) % RING, q, it * 2 + 1)
                second(n0 + N_FFN - 2, (n0 + N_FFN - 2) % RING, FG, last=True)
                norm_rest(2 * layer + 2)

            norm_start(1)
            norm_rest(1)
            ffn("f0", 0, AT_F0)

            project("inc", AT_INC, KT, after_norm=2)
            for e in range(4):
                n, g = AT_GRP + e // 2, POOL_ORDER[2 * e] // 2
                pe.wait_ge(dl_done, 2 * e + 2)
                for m in range(2):
                    pe.wait_ge(free["grp"], 2 * e + m + 1)
                    tile(n, n % RING, m, "grp", col=(e % 2) * 512 + m * 256, ks=range(2 * g, 2 * g + 2),
                         release=(e % 2 == 1 and m == 1))
            pe.wait_ge(zl_done, 8)
            project("outc", AT_OUTC, KT)
            norm_start(3)
            norm_rest(3)
            ffn("f1", 1, AT_F1)

        @block.scalar
        def _(act):
            for s in free.values():
                act.sem_inc(s, 2)
            for s in set_free.values():
                act.sem_inc(s[0], 1)

            def banks(s):
                return PS[:, 3 * s:3 * s + 3, 0:CH]

            def chunks(ap):
                return ap.rearrange("p (c t) -> p c t", c=NCH)

            for s in range(RING):
                act.dma_start(RAW[:, s, :], wst[s]).then_inc(raw_loaded[s], 16)
            for k in range(KT):
                act.wait_ge(x_loaded[k], 16)
                act.activation(XH[:, k, :], XRAW[:, k, :], ACT.Copy).then_inc(x_hi, 1)

            rots = sgs = 0
            act.wait_ge(hist_loaded, 16 * CT)
            for n, name in enumerate(IN_ORDER):
                src = banks(n % 2)
                act.wait_ge(full["in"], n + 1)
                if name in ("ks", "kw") or name[0] == "q":
                    dst = QT[:, int(name[1]), :] if name[0] == "q" else kv(name)
                    act.activation(chunks(dst), src, ACT.Copy).then_inc(rot_full, 1)
                    if rots:
                        act.wait_ge(rot_free, rots)
                    for q in range(4):
                        o = q ^ 1
                        ins = act.activation(chunks(ROT[32 * q:32 * q + 32, :]), src[32 * o:32 * o + 32], ACT.Copy)
                        ins.then_inc(rot_full, 1)
                    rots += 1
                    act.wait_ge(rot_full, 5 * rots)
                elif name[:2] == "gb":
                    if sgs:
                        act.wait_ge(sg_free, sgs)
                    sgs += 1
                    act.activation(chunks(SG[:, :]), src, ACT.Sigmoid).then_inc(sg_full, 1)
                    act.wait_ge(sg_full, sgs)
                elif name[:2] == "ga":
                    c = int(name[2])
                    act.activation(UE[:, c, CW - 1:CW - 1 + 2 * CH].rearrange("p (c t) -> p c t", c=2), src[:, 0:2, :], ACT.Copy).then_inc(ga_full, 1)
                    act.activation(UE[:, c, CW - 1 + 2 * CH:UEP], src[:, 2, 0:LAST], ACT.Copy).then_inc(ga_full, 1)
                    act.activation(UE[:, c, UEP:].rearrange("p (b u) -> p b u", b=SB)[:, :, CW - 1:],
                                   src[:, 2, LAST:LAST + SB * SS].rearrange("p (b s) -> p b s", b=SB), ACT.Copy).then_inc(ga_full, 1)
                    act.wait_ge(ga_full, 3 * (c + 1))
                elif name == "gl":
                    act.wait_ge(sg_free, CT)
                    act.activation(chunks(GT[0:24, :]), src[0:24], ACT.Sigmoid).then_inc(gl_done, 1)
                    act.wait_ge(gl_done, 1)
                else:
                    act.activation(chunks(kv(name)), src, ACT.Copy).then_inc(kv_evac, 1)
                    act.wait_ge(kv_evac, {"kc": 1, "vc": 2, "vs": 3, "vw": 4}[name])
                    if name in ("kc", "vc"):
                        act.dma_start(kvT[KV_AT[name]], kv(name)).then_inc(kc_stored, 16)
                act.sem_inc(free["in"], 1)

            act.wait_ge(c_loaded, 5 * 16)
            act.wait_ge(kc_stored, 16 * 2)
            for kind in range(2):
                act.dma_start(KV4[:, kind, NP_TOK:NP_TOK + NB], pe_t[:, kind]).then_inc(pe_loaded, 16)
            for job in range(4):
                page_loads(act, job, 1)

            act.wait_ge(job_done, 4)
            act.dma_start(SMC[:, :], smp_c).then_inc(smp_c_loaded, 16)
            sample_windows(act, 0)

            for n, (srcs, dst, rows) in enumerate(TURNS):
                act.wait_ge(turned, n + 1)
                if n == 0:
                    act.wait_ge(kv_stored, 9 * 16)
                    act.wait_ge(job_done, 4)
                act.activation(dst, PS[0:rows, 4 + n % 2, 0:4 * P].rearrange("p (j t) -> p j t", j=4), ACT.Copy).then_inc(turned_out, 1)
            act.wait_ge(turned, T_GATE + 1)
            act.activation(GN[:, :, :].rearrange("p i n -> p (i n)"), PS[:, 4 + T_GATE % 2, 0:QT_N * 24], ACT.Copy).then_inc(turned_out, 1)
            act.wait_ge(turned, T_VBD + 1)
            act.wait_ge(vbd_zero, 1)
            for g in range(G):
                for r in range(R):
                    ins = act.activation(VBD[32 * r:32 * r + 32, g, r * HD:(r + 1) * HD],
                                         PS[0:NB, 4 + T_VBD % 2, g * HD:(g + 1) * HD], ACT.Copy)
                    ins.then_inc(vbd_in, 1)
            act.wait_ge(vbd_in, G * R)
            act.sem_inc(turned_out, 1)

            turn = 0
            for gi in range(4):
                act.wait_ge(s_cexp_in, gi + 1)
                act.activation(ST[:, 32:64], ST[:, 0:32], ACT.Exp, scale=SCALE).then_inc(s_cexp, 1)

                def move(dsts):
                    nonlocal turn
                    act.wait_ge(s_turn, turn + 1)
                    for dst, src in dsts:
                        ins = act.activation(dst, src, ACT.Copy)
                    ins.then_inc(s_turned, 1)
                    turn += 1

                for kind in range(2):
                    act.wait_ge(s_masked, 2 * gi + kind + 1)
                    n = (W_HIST, 8 * P)[kind] + SS
                    act.activation(PB[:, kind, 0:n], PB[:, kind, 0:n], ACT.Exp, bias=ST[:, 200 + kind:201 + kind], scale=SCALE,
                                   accum_out=ST[:, 204 + kind:205 + kind]).then_inc(s_exp, 1)
                    if kind == 0:
                        if gi:
                            act.wait_ge(s_pv, 3 * gi)
                        move([(PTB[0:NB, 0, 0:P], PS[0:NB, 6, 0:P])])
                        act.wait_ge(s_pv, 3 * gi + 1)
                        move([(PTB[:, 0, 0:4 * P], PS[:, 6, 0:4 * P])])
                        move([(PTB[0:SS, 0, 4 * P:5 * P], PS[0:SS, 6, 0:P])])
                    else:
                        act.wait_ge(s_pv, 3 * gi + 2)
                        move([(PTB[:, 0, 0:4 * P], PS[:, 6, 0:4 * P])])
                        move([(PTB[:, 1, 0:4 * P], PS[:, 6, 0:4 * P])])
                        move([(PTB[0:SS, 0, 4 * P:5 * P], PS[0:SS, 6, 0:P])])

            def split_high(n):
                src, hi, _ = SPLITS[n]
                act.activation(hi, src, ACT.Copy).then_inc(q_hi, 1)

            def conv_norm():
                act.wait_ge(s_ms, 4)
                act.wait_ge(s_outT, 4)
                for n in range(R):
                    split_high(n)
                for c in range(NCH):
                    act.wait_ge(ln_cent, c + 1)
                    if c:
                        act.wait_ge(ln_var, c)
                    act.activation(SQC[:, :, :], CA[:, :, c * CH:(c + 1) * CH], ACT.Square).then_inc(ln_sq, 1)
                    split_high(R + c)
                for c in range(NCH):
                    act.wait_ge(ln_ve, c + 1)
                    act.activation(RSC[:, c, :], RSC[:, c, :], ACT.Sqrt).then_inc(ln_sqrt, 1)

            def wide_norm(L, g_at, last=False):
                b = NCH * L
                bias = PR_LN + g_at + KT

                def square(c):
                    act.wait_ge(ln_cent, b + c + 1)
                    act.wait_ge(ln_var, b + c)
                    act.activation(SQ[:, :, :], Y[:, :, c * CH:(c + 1) * CH], ACT.Square).then_inc(ln_sq, 1)

                def root(c):
                    act.wait_ge(ln_ve, b + c + 1)
                    act.activation(RS[:, c % 2, :], RS[:, c % 2, :], ACT.Sqrt).then_inc(ln_sqrt, 1)

                def high(c):
                    for k in range(KT):
                        act.wait_ge(wn_scaled, KT * (b - NCH + c) + k + 1)
                        act.activation(XH[:, k, c * CH:(c + 1) * CH], Y[:, k, c * CH:(c + 1) * CH], ACT.Identity,
                                       bias=PR[:, bias + k:bias + k + 1]).then_inc(wn_hi, 1)

                def whole(c):
                    for k in range(KT):
                        act.wait_ge(wn_scaled if last else wn_lo, KT * ((b - NCH) + c) + k + 1)
                        y = Y[:, k, c * CH:(c + 1) * CH]
                        act.activation(y, y, ACT.Identity, bias=PR[:, bias + k:bias + k + 1]).then_inc(wn_y, 1)

                square(0)
                square(1)
                root(0)
                if last:
                    square(2)
                    whole(0)
                    root(1)
                    whole(1)
                    root(2)
                    whole(2)
                    return
                high(0)
                square(2)
                root(1)
                whole(0)
                high(1)
                root(2)
                whole(1)
                high(2)
                whole(2)

            conv_norm()
            act.wait_ge(s_ms, 4)
            act.activation(XH[:, 0:4, NP_TOK:T], MS[:, :, :], ACT.Copy).then_inc(ms_hi, 1)

            def exps(n):
                i, g, kind, r, k0, nk = units[n]
                act.wait_ge(p_masked, n + 1)
                at = 208 + 8 * (n // GU % 2) + 4 * (kind == "sel") + r
                act.activation(PB[:, n % 2, 0:nk * P], PB[:, n % 2, 0:nk * P], ACT.Exp, bias=ST[:, 224 + n % 2:225 + n % 2],
                               scale=-1.0, accum_out=ST[:, at:at + 1]).then_inc(p_exp, 1)

            def cmp_exps(n):
                act.wait_ge(p_cin, n // GU + 1)
                act.activation(ST[:, 0:P], ST[:, 0:P], ACT.Exp, scale=SCALE).then_inc(p_cexp, 1)

            def second_half(n):
                if units[n][5] > first[n]:
                    act.wait_ge(p_t1, t1_upto[n + 1])
                    if buffer_read(n):
                        act.wait_ge(p_pv, buffer_read(n))
                    act.activation(PTB[:, n % 2, first[n] * P:units[n][5] * P], PS[:, 5, 0:(units[n][5] - first[n]) * P],
                                   ACT.Copy).then_inc(p_c1, 1)

            def out_high(i):
                act.wait_ge(p_ot, i + 1)
                act.activation(XH[:, 0:4, i * P:(i + 1) * P], PS[:, 5, :].rearrange("p (r q) -> p r q", r=R), ACT.Copy).then_inc(p_ohi, 1)

            cmp_exps(0)
            for n, u in enumerate(units):
                second_half(n)
                if n + 1 < len(units) and units[n + 1][2] != "cmp":
                    exps(n + 1)
                if n + 2 < len(units) and units[n + 2][2] == "cmp":
                    cmp_exps(n + 2)
                if u[0] and n % (2 * GU) == OUT_AT:
                    out_high(u[0] - 1)
            act.wait_ge(ln_norm, NCH)
            for c in range(CT):
                act.activation(CA[:, c, :], CA[:, c, :], ACT.Silu).then_inc(cv_act, 1)
            act.wait_ge(cv_act, CT)
            act.wait_ge(p_pv, len(units))
            for c in range(CT):
                act.activation(XH[:, 4 + c, :], CA[:, c, :], ACT.Copy).then_inc(cv_hi, 1)
            out_high(QT_N - 1)

            def ffn(st):
                def pair(it, first_pair):
                    for q in range(2):
                        act.wait_ge(full[st], it * 4 + (2 * q + 1))
                        if q or not first_pair:
                            act.wait_ge(ht_done[1 - q], it * 1 + q + ht_base[0])
                        act.activation(chunks(SL[:, :]), banks(0), ACT.Silu).then_inc(silu_done[q], 1)
                        act.wait_ge(silu_done[q], it + (1 + ht_base[0]))
                        act.sem_inc(set_free[st][0], 1)
                        act.wait_ge(ht_done[q], it + (1 + ht_base[0]))
                        if not first_pair:
                            act.wait_ge(y_full[1], it * 12 + 12 * ht_base[0])
                        act.activation(HH[:, q, :], HT[:, q, :], ACT.Copy).then_inc(hh_done[q], 1)

                pair(0, True)
                with act.Fori(1, FG) as it:
                    pair(it, False)
                ht_base[0] += FG

            ht_base = [0]
            wide_norm(1, 0)
            ffn("f0")
            wide_norm(2, 16)

            act.wait_ge(wn_lo, KT * NCH * 2)
            for m in range(KT):
                act.dma_start(UP[:, m, PUP:].rearrange("p (b u) -> p b u", b=SB)[:, :, 0:PH],
                              hist_p[:, m]).then_inc(hp_loaded, 16)
            act.dma_start(INV[:, :, :], invc).then_inc(inv_loaded, 16)
            act.wait_ge(hp_loaded, 16 * KT)
            for e, m in enumerate(POOL_ORDER):
                src = banks(e % 2)
                act.wait_ge(full["inc"], e + 1)
                act.activation(UP[:, m, PH:PH + 2 * CH].rearrange("p (c t) -> p c t", c=2), src[:, 0:2, :], ACT.Copy).then_inc(up_in, 1)
                act.activation(UP[:, m, PH + 2 * CH:PUP], src[:, 2, 0:LAST], ACT.Copy).then_inc(up_in, 1)
                act.activation(UP[:, m, PUP:].rearrange("p (b u) -> p b u", b=SB)[:, :, PH:],
                               src[:, 2, LAST:LAST + SB * SS].rearrange("p (b s) -> p b s", b=SB), ACT.Copy).then_inc(up_in, 1)
                act.wait_ge(up_in, 5 * e + 3)
                act.sem_inc(free["inc"], 1)
                act.activation(POUT[:, m, 0, :], UP[:, m, NP_TOK:PUP], ACT.Copy).then_inc(up_in, 1)
                act.activation(POUT[:, m, 1:, :], UP[:, m, PUP:].rearrange("p (b u) -> p b u", b=SB)[:, :, SS:], ACT.Copy).then_inc(up_in, 1)
            act.wait_ge(up_in, 5 * KT)
            act.dma_start(poolT, POUT[:, :, :, :]).then_inc(stored, 16)
            for e, m in enumerate(POOL_ORDER):
                act.wait_ge(d_done, 2 * (e + 1))
                act.wait_ge(full["inc"], KT)
                act.activation(XH[:, m, 0:NP_TOK], UP[:, m, PH:PUP], ACT.Copy).then_inc(dh_done, 1)
                act.activation(XH[:, m, NP_TOK:T].rearrange("p (b s) -> p b s", b=SB),
                               UP[:, m, PUP:].rearrange("p (b u) -> p b u", b=SB)[:, :, PH:], ACT.Copy).then_inc(dh_done, 1)
            for e, m in enumerate(POOL_ORDER):
                act.wait_ge(full["grp"], 2 * (e // 2) + 2)
                act.activation(chunks(XH[:, m, :]), banks(e % 2), ACT.Identity, scale=PR[:, PR_SC + m:PR_SC + m + 1]).then_inc(zh_done, 1)
            wide_norm(3, 32)
            ffn("f1")
            wide_norm(4, 48, last=True)
            for c in range(NCH):
                act.wait_ge(wn_y, KT * (3 * NCH + c + 1))
                act.dma_start(yT[:, :, c * CH:(c + 1) * CH], Y[:, :, c * CH:(c + 1) * CH]).then_inc(stored, 16)
            act.wait_ge(stored, 16 * (1 + 1 + NCH))
            act.wait_ge(kv_stored, 9 * 16)

        @block.vector
        def _(dve):
            chain = [0]

            def link(ins):
                chain[0] += 1
                ins.then_inc(dv, 1)
                dve.wait_ge(dv, chain[0])

            def banks(s):
                return PS[:, 3 * s:3 * s + 3, 0:CH]

            def chunks(ap):
                return ap.rearrange("p (c t) -> p c t", c=NCH)

            for s in set_free.values():
                dve.sem_inc(s[1], 1)
            dve.memset(UE[:, :, 0:CW - 1], 0.0).then_inc(ue_zeroed, 1)
            for k in range(KT):
                dve.wait_ge(x_hi, k + 1)
                dve.tensor_tensor(XL[:, k, :], XRAW[:, k, :], XHf[:, k, :], ALU.subtract).then_inc(x_split, 1)
            dve.wait_ge(c_loaded, 5 * 16)

            rots = [0]

            def rope(dst):
                rots[0] += 1
                dve.wait_ge(rot_full, 5 * rots[0])
                dve.tensor_tensor(dst, dst, COS[:, :], ALU.mult).then_inc(dv, 1)
                dve.tensor_tensor(ROT[:, :], ROT[:, :], SIN[:, :], ALU.mult).then_inc(dv, 1)
                chain[0] += 2
                dve.wait_ge(dv, chain[0])
                dve.tensor_tensor(dst, dst, ROT[:, :], ALU.add).then_inc(roped, 1)
                dve.wait_ge(roped, rots[0])
                dve.sem_inc(rot_free, 1)

            def gate(c):
                dve.wait_ge(sg_full, c + 1)
                dve.wait_ge(ga_full, 3 * (c + 1))
                dve.tensor_tensor(UE[:, c, CW - 1:UEP], UE[:, c, CW - 1:UEP], SG[:, 0:NP_TOK], ALU.mult).then_inc(dv, 1)
                s = UE[:, c, UEP:].rearrange("p (b u) -> p b u", b=SB)[:, :, CW - 1:]
                dve.tensor_tensor(s, s, SG[:, NP_TOK:T].rearrange("p (b s) -> p b s", b=SB), ALU.mult).then_inc(dv, 1)
                chain[0] += 2
                dve.wait_ge(dv, chain[0])
                dve.sem_inc(sg_free, 1)
                dve.sem_inc(gated, 1)

            def conv(c, taps):
                for j in taps:
                    w = PR[:, PR_CW + c * CW + j:PR_CW + c * CW + j + 1]
                    parts = [(CA[:, c, 0:NP_TOK], UE[:, c, j:j + NP_TOK]),
                             (CA[:, c, NP_TOK:T].rearrange("p (b s) -> p b s", b=SB),
                              UE[:, c, UEP:].rearrange("p (b u) -> p b u", b=SB)[:, :, j:j + SS])]
                    for q, (dst, src) in enumerate(parts):
                        if j == 0:
                            dve.tensor_scalar(dst, src, w, PR[:, PR_CB + c:PR_CB + c + 1], ALU.mult, ALU.add).then_inc(conv_step, 1)
                        else:
                            dve.wait_ge(conv_step, 2 * (c * CW + j) + q - 1)
                            dve.scalar_tensor_tensor(out=dst, in0=src, scalar=w, in1=dst, op0=ALU.mult, op1=ALU.add).then_inc(conv_step, 1)

            dve.memset(CA[:, :, T:TP], 0.0).then_inc(ue_zeroed, 1)
            dve.wait_ge(ue_zeroed, 2)
            dve.wait_ge(hist_loaded, 16 * CT)
            rope(kv("ks"))
            rope(kv("kw"))
            gate(0)
            conv(0, range(CW))
            gate(1)
            conv(1, range(CW))
            gate(2)
            conv(2, range(0, 12))
            rope(QT[:, 0, :])
            conv(2, range(12, 20))
            rope(QT[:, 1, :])
            conv(2, range(20, CW))
            gate(3)
            rope(QT[:, 2, :])
            conv(3, range(0, 8))
            rope(QT[:, 3, :])
            conv(3, range(8, CW))

            dve.wait_ge(conv_step, 2 * CW * CT)
            dve.wait_ge(job_done, 4)
            dve.wait_ge(kv_stored, 9 * 16)
            dve.wait_ge(smp_c_loaded, 16)
            dve.wait_ge(att_c_loaded, 16)
            dve.memset(VBD[:, :, :], 0.0).then_inc(vbd_zero, 1)
            link(dve.tensor_copy(QS[:, :, :, :].rearrange("p b r s -> p r b s"),
                                 QT[:, :, NP_TOK:T].rearrange("p r (b s) -> p r b s", b=SB)))
            nkc = NB * (1 + SB)
            for kind in range(2):
                link(dve.tensor_copy(ST[:, 250 + kind:251 + kind], PS[:, kind, nkc + NB:nkc + NB + 1]))
            for kind in range(2):
                bias = ST[:, 250 + kind:251 + kind]
                link(dve.tensor_scalar(KR[:, kind, 0:NB], PS[:, kind, nkc:nkc + NB], bias, None, ALU.add))
                link(dve.tensor_scalar(KR[:, kind, NB:nkc], PS[:, kind, NB:nkc], bias, None, ALU.add))
            dve.sem_inc(kr_done, 1)
            rotc = PB[:, 0, 0:nkc]
            for q in range(4):
                o = q ^ 1
                link(dve.tensor_copy(PB[32 * q:32 * q + 32, 0, 0:nkc], KR[32 * o:32 * o + 32, 0, :]))
            link(dve.tensor_tensor(KCT[:, :], KR[:, 0, :], SMC[:, SC_COS:SC_COS + nkc], ALU.mult))
            link(dve.tensor_tensor(rotc, rotc, SMC[:, SC_SIN:SC_SIN + nkc], ALU.mult))
            dve.tensor_tensor(KCT[:, :], KCT[:, :], rotc, ALU.add).then_inc(kct_done, 1)
            dve.wait_ge(kct_done, 1)
            dve.wait_ge(turned_out, N_TURNS)
            dve.wait_ge(g_in, 16 * 16)

            for gi in range(4):
                dve.wait_ge(s_cmp, gi + 1)
                if gi:
                    dve.wait_ge(s_pv, 3 * gi)
                sc = ST[:, 0:32]
                link(dve.tensor_reduce(ST[:, 190:191], PS[:, 5, 0:NB], AX.X, ALU.max))
                dve.tensor_scalar(sc, PS[:, 5, 0:NB], ST[:, 190:191], None, ALU.subtract).then_inc(s_cexp_in, 1)
                dve.wait_ge(s_cexp, gi + 1)
                link(dve.tensor_reduce(ST[:, 191:192], ST[:, 32:64], AX.X, ALU.add))
                link(dve.reciprocal(ST[:, 191:192], ST[:, 191:192]))
                dve.tensor_scalar(ST[:, 64:96], ST[:, 32:64], ST[:, 191:192], None, ALU.mult).then_inc(s_pc, 1)
                dve.wait_ge(s_win, gi + 1)
                if gi:
                    dve.wait_ge(s_turned, 6 * gi)

                def masked(kind, parts):
                    for n, (dst, src, mask) in enumerate(parts):
                        link(dve.tensor_tensor_reduce(dst, src, mask, 1.0, -3.0e38, ALU.add, ALU.max, ST[:, 192 + n:193 + n]))
                    link(dve.tensor_tensor(ST[:, 194:195], ST[:, 192:193], ST[:, 193:194], ALU.max))
                    dve.tensor_scalar(ST[:, 200 + kind:201 + kind], ST[:, 194:195], -SCALE, None, ALU.mult).then_inc(s_masked, 1)
                    dve.wait_ge(s_masked, 2 * gi + kind + 1)

                masked(0, [(PB[:, 0, 0:W_HIST], PS[:, 0, :], SMC[:, SC_WM:SC_WM + W_HIST]),
                           (PB[:, 0, W_HIST:W_HIST + SS], PS[:, 1, 0:SS], SMC[:, SC_WM + W_HIST:SC_WM + W_HIST + SS])])
                dve.wait_ge(s_imp, gi + 1)
                link(dve.memset(ST[:, 128:145], 0.0))
                link(dve.tensor_reduce(ST[:, 128:144], PS[:, 5, 64:64 + NB].rearrange("p (b t) -> p b t", t=2), AX.X, ALU.add))
                link(dve.tensor_tensor(ST[:, 128:145], ST[:, 128:145], SMC[:, SC_SB:SC_SB + 17], ALU.add))
                link(dve.max(ST[:, 150:158], ST[:, 128:145]))
                link(dve.match_replace(ST[:, 160:177], ST[:, 150:158], ST[:, 128:145], TAKEN))
                link(dve.tensor_scalar(ST[:, 160:176], ST[:, 160:176], TAKEN, -1.0, ALU.is_equal, ALU.add))
                link(dve.tensor_scalar(ST[:, 160:176], ST[:, 160:176], BIG, None, ALU.mult))
                dve.wait_ge(s_sel, gi + 1)
                masked(1, [(PB[:, 1, 0:8 * P].rearrange("p (b t) -> p b t", t=64),
                            PS[:, 2:4, :].rearrange("p a (b t) -> p (a b) t", t=64),
                            ST[:, 160:176, None].to_broadcast([P, 16, 64])),
                           (PB[:, 1, 8 * P:8 * P + SS], PS[:, 4, 0:SS], SMC[:, SC_NEW:SC_NEW + SS])])
                dve.wait_ge(s_exp, 2 * gi + 2)
                link(dve.reciprocal(ST[:, 204:206], ST[:, 204:206]))
                link(dve.tensor_tensor(ST[:, 204:206], ST[:, 204:206], GNS[:, gi, 2:0:-1], ALU.mult))
                dve.wait_ge(s_pv, 3 * gi + 3)
                o = OC[:, 0, 0, :]
                link(dve.tensor_scalar(o, PS[:, 7, 0:HD], GNS[:, gi, 0:1], None, ALU.mult))
                link(dve.scalar_tensor_tensor(out=o, in0=PS[:, 7, HD:2 * HD], scalar=ST[:, 204:205], in1=o, op0=ALU.mult, op1=ALU.add))
                dve.scalar_tensor_tensor(out=o, in0=PS[:, 7, 2 * HD:3 * HD], scalar=ST[:, 205:206], in1=o, op0=ALU.mult, op1=ALU.add).then_inc(s_mixed, 1)
                dve.wait_ge(s_outT, gi + 1)
                for g in range(G):
                    for bb in range(2):
                        at = (2 * gi + bb) * SS
                        src = PS[0:HD, 5, 128 + 32 * (2 * bb + g):128 + 32 * (2 * bb + g) + 32]
                        link(dve.tensor_copy(MS[g * HD:(g + 1) * HD, :, at:at + SS], src.rearrange("p (r s) -> p r s", r=R)))
                dve.sem_inc(s_ms, 1)

            def centre(x, nk, b, c):
                dve.wait_ge(ln_mean, b + c + 1)
                mean = PS[:, c:c + 1, 0:CH].to_broadcast([P, nk, CH])
                dve.tensor_tensor(x, x, mean, ALU.subtract).then_inc(ln_cent, 1)

            def conv_norm():
                for c in range(NCH):
                    centre(CA[:, :, c * CH:(c + 1) * CH], CT, 0, c)
                for n, (src, hi, lo) in enumerate(SPLITS):
                    dve.wait_ge(q_hi, n + 1)
                    dve.tensor_tensor(lo, src, hi.bitcast(F32), ALU.subtract).then_inc(q_lo, 1)
                for c in range(NCH):
                    dve.wait_ge(ln_var, c + 1)
                    dve.tensor_scalar(RSC[:, c, :], PS[:, 3 + c, 0:CH], EPS, None, ALU.add).then_inc(ln_ve, 1)
                dve.wait_ge(ln_cent, NCH)

            def conv_scale(step):
                c, part = step // CONV_STEPS, step % CONV_STEPS
                x = CA[:, :, c * CH:(c + 1) * CH]
                if part == 0:
                    dve.wait_ge(ln_sqrt, c + 1)
                    link(dve.reciprocal(RSC[:, c, :], RSC[:, c, :]))
                elif part == 1:
                    link(dve.tensor_tensor(x, x, RSC[:, c:c + 1, :].to_broadcast([P, CT, CH]), ALU.mult))
                else:
                    for k in range(CT):
                        dve.tensor_scalar(x[:, k, :], x[:, k, :], PR[:, PR_CG + k:PR_CG + k + 1], PR[:, PR_CN + k:PR_CN + k + 1],
                                          ALU.mult, ALU.add).then_inc(dv, 1)
                    chain[0] += CT
                    dve.wait_ge(dv, chain[0])
                    dve.sem_inc(ln_norm, 1)

            def wide_centre(L, c):
                centre(Y[:, :, c * CH:(c + 1) * CH], KT, NCH * L, c)

            def wide_norm(L, g_at, started=False, last=False):
                b = NCH * L
                gain, bias = PR_LN + g_at, PR_LN + g_at + KT

                def plus_eps(c):
                    dve.wait_ge(ln_var, b + c + 1)
                    dve.tensor_scalar(RS[:, c % 2, :], PS[:, 3 + c, 0:CH], EPS, None, ALU.add).then_inc(ln_ve, 1)

                def scale(c):
                    dve.wait_ge(ln_sqrt, b + c + 1)
                    link(dve.reciprocal(RS[:, c % 2, :], RS[:, c % 2, :]))
                    dve.wait_ge(ln_cent, b + c + 1)
                    for k in range(KT):
                        y = Y[:, k, c * CH:(c + 1) * CH]
                        dve.scalar_tensor_tensor(out=y, in0=y, scalar=PR[:, gain + k:gain + k + 1], in1=RS[:, c % 2, :],
                                                 op0=ALU.mult, op1=ALU.mult).then_inc(wn_scaled, 1)

                def low(c):
                    dve.wait_ge(wn_scaled, KT * (b - NCH + c + 1))
                    for k in range(KT):
                        at = slice(c * CH, (c + 1) * CH)
                        dve.wait_ge(wn_hi, KT * (b - NCH + c) + k + 1)
                        dve.scalar_tensor_tensor(out=XL[:, k, at], in0=Y[:, k, at], scalar=PR[:, bias + k:bias + k + 1],
                                                 in1=XHf[:, k, at], op0=ALU.add, op1=ALU.subtract).then_inc(wn_lo, 1)

                if not started:
                    wide_centre(L, 0)
                    wide_centre(L, 1)
                plus_eps(0)
                scale(0)
                wide_centre(L, 2)
                for c in range(NCH):
                    if c + 1 < NCH:
                        plus_eps(c + 1)
                    if not last:
                        low(c)
                    if c + 1 < NCH:
                        scale(c + 1)

            dve.wait_ge(s_exp, 8)
            dve.sem_inc(ln_in, NCH)
            conv_norm()
            dve.wait_ge(ms_hi, 1)
            link(dve.tensor_tensor(XL[:, 0:4, NP_TOK:T], MS[:, :, :], XHf[:, 0:4, NP_TOK:T], ALU.subtract))
            link(dve.memset(XH[:, 0:4, T:TP].bitcast(F32), 0.0))
            link(dve.memset(XL[:, 0:4, T:TP].bitcast(F32), 0.0))

            def cmp_probs(n):
                i, m = units[n][0], n // GU
                b = 2 * (n % 2)
                dve.wait_ge(p_scores, n + 1)
                sc = ST[:, 0:P].rearrange("p (r n) -> p r n", r=R)
                cma = ATC[:, AC_CMA + i * NB:AC_CMA + (i + 1) * NB]
                cmm = ATC[:, AC_CMM + i * NB:AC_CMM + (i + 1) * NB]
                if m:
                    dve.wait_ge(p_t0, n - GU + 1)
                dve.tensor_tensor(sc, PS[:, b, 0:P].rearrange("p (r n) -> p r n", r=R),
                                  cma[:, None, :].to_broadcast([P, R, NB]), ALU.add).then_inc(p_masked, 1)
                dve.wait_ge(p_masked, n + 1)
                link(dve.tensor_reduce(ST[:, 128:132], sc, AX.X, ALU.max))
                dve.tensor_tensor(sc, sc, ST[:, 128:132, None].to_broadcast([P, R, NB]), ALU.subtract).then_inc(p_cin, 1)
                dve.wait_ge(p_cexp, m + 1)
                link(dve.tensor_tensor(sc, sc, cmm[:, None, :].to_broadcast([P, R, NB]), ALU.mult))
                link(dve.tensor_reduce(ST[:, 128:132], sc, AX.X, ALU.add))
                link(dve.tensor_scalar(ST[:, 128:132], ST[:, 128:132], TINY, None, ALU.max))
                link(dve.reciprocal(ST[:, 128:132], ST[:, 128:132]))
                dve.tensor_tensor(sc, sc, ST[:, 128:132, None].to_broadcast([P, R, NB]), ALU.mult).then_inc(p_cpc, 1)
                dve.wait_ge(p_cpc, m + 1)

            def select(n):
                i = units[n][0]
                link(dve.tensor_reduce(ST[:, 136:152], ST[:, 0:P].rearrange("p (r b t) -> p b r t", r=R, t=2), AX.XY, ALU.add))
                link(dve.tensor_tensor(ST[:, 136:152], ST[:, 136:152], ATC[:, AC_SB + i * 16:AC_SB + (i + 1) * 16], ALU.add))
                link(dve.max(ST[:, 152:160], ST[:, 136:152]))
                link(dve.match_replace(ST[:, 160:176], ST[:, 152:160], ST[:, 136:152], TAKEN))
                link(dve.tensor_scalar(ST[:, 160:176], ST[:, 160:176], TAKEN, -1.0, ALU.is_equal, ALU.add))
                w = 2 * (i + 1)
                link(dve.tensor_scalar(SMASK[:, 0:w * 64].rearrange("p (b t) -> p b t", t=64),
                                       ST[:, 160:160 + w, None].to_broadcast([P, w, 64]), BIG, None, ALU.mult))
                d = SMASK[:, i * P:(i + 1) * P]
                link(dve.tensor_tensor(d, d, ATC[:, AC_CAUS:AC_CAUS + P], ALU.add))

            def mask(n):
                i, g, kind, r, k0, nk = units[n]
                b = 2 * (n % 2)
                dve.wait_ge(p_scores, n + 1)
                if n >= 2:
                    dve.wait_ge(p_t0, n - 1)
                    if t1_upto[n - 1]:
                        dve.wait_ge(p_t1, t1_upto[n - 1])
                w = nk * P
                msk = SMASK[:, 0:w] if kind == "sel" else ATC[:, AC_WM + 640 - w:AC_WM + 640]
                src = PS[:, b, 0:w] if w <= 512 else PS[:, b:b + 2, :].rearrange("p a t -> p (a t)")[:, 0:w]
                dve.tensor_tensor_reduce(PB[:, n % 2, 0:w], src, msk, -SCALE, 3.0e38, ALU.add, ALU.min,
                                         ST[:, 224 + n % 2:225 + n % 2]).then_inc(p_masked, 1)

            def first_half(n):
                dve.wait_ge(p_t0, n + 1)
                if units[n][2] == "cmp":
                    if n:
                        dve.wait_ge(p_pv, n - GU + 1)
                    dve.tensor_copy(PTC[:, :], PS[:, 4, 0:P]).then_inc(p_c0, 1)
                    return
                if buffer_read(n):
                    dve.wait_ge(p_pv, buffer_read(n))
                dve.tensor_copy(PTB[:, n % 2, 0:first[n] * P], PS[:, 4, 0:first[n] * P]).then_inc(p_c0, 1)

            def mix(m):
                i, g = m // G, m % G
                n = last_of[(i, g)]
                den = ST[:, 208 + 8 * (m % 2):216 + 8 * (m % 2)]
                gates = GN[:, i, g * 12:(g + 1) * 12].rearrange("p (r b) -> p b r", b=3)
                dve.wait_ge(p_exp, big_upto[n + 1])
                link(dve.reciprocal(ST[:, 240:248], den))
                link(dve.tensor_tensor(ST[:, 240:244], ST[:, 240:244], gates[:, 2, :], ALU.mult))
                link(dve.tensor_tensor(ST[:, 244:248], ST[:, 244:248], gates[:, 1, :], ALU.mult))
                if i and g == 0:
                    dve.wait_ge(p_ot, i)
                dve.wait_ge(p_pv, n + 1)
                o = OC[:, :, g, :]
                t = OTMP[:, :].rearrange("p (r d) -> p r d", r=R)

                def branch(bank, col):
                    return PS[:, bank, col:col + R * HD].rearrange("p (r d) -> p r d", r=R)

                link(dve.tensor_tensor(o, branch(6, 0), gates[:, 0, :, None].to_broadcast([P, R, HD]), ALU.mult))
                link(dve.tensor_tensor(t, branch(6, R * HD), ST[:, 240:244, None].to_broadcast([P, R, HD]), ALU.mult))
                link(dve.tensor_tensor(o, o, t, ALU.add))
                link(dve.tensor_tensor(t, branch(7, 0), ST[:, 244:248, None].to_broadcast([P, R, HD]), ALU.mult))
                dve.tensor_tensor(o, o, t, ALU.add).then_inc(p_mixed, 1)
                dve.wait_ge(p_mixed, m + 1)

            def out_low(i):
                dve.wait_ge(p_ohi, i + 1)
                dve.tensor_tensor(XL[:, 0:4, i * P:(i + 1) * P], PS[:, 5, :].rearrange("p (r q) -> p r q", r=R),
                                  XHf[:, 0:4, i * P:(i + 1) * P], ALU.subtract).then_inc(p_olo, 1)

            dve.wait_ge(q_lo, len(SPLITS))
            cmp_probs(0)
            select(0)
            side = 0
            for n, u in enumerate(units):
                if n + 1 < len(units) and units[n + 1][2] != "cmp":
                    mask(n + 1)
                first_half(n)
                if n > GU and units[n - 1][2] == "cmp":
                    mix(n // GU - 1)
                if n + 1 < len(units) and units[n + 1][2] == "cmp":
                    select(n + 1)
                if n + 2 < len(units) and units[n + 2][2] == "cmp":
                    cmp_probs(n + 2)
                if u[0] and n % (2 * GU) == OUT_AT:
                    out_low(u[0] - 1)
                if u[0] >= QT_N - 4 and n % GU in (3, 5) and side < NCH * CONV_STEPS:
                    conv_scale(side)
                    side += 1
            assert side == NCH * CONV_STEPS
            mix(G * QT_N - 1)
            for c in range(CT):
                dve.wait_ge(cv_hi, c + 1)
                dve.tensor_tensor(XL[:, 4 + c, :], CA[:, c, :], XHf[:, 4 + c, :], ALU.subtract).then_inc(cv_lo, 1)
            out_low(QT_N - 1)

            def residual(st, ln):
                for m in range(KT):
                    dve.wait_ge(full[st], m + 1)
                    y = chunks(Y[:, m, :])
                    dve.scalar_tensor_tensor(out=y, in0=y, scalar=ALPHA, in1=banks(m % 2), op0=ALU.mult, op1=ALU.add).then_inc(dv, 1)
                    chain[0] += 1
                    dve.wait_ge(dv, chain[0])
                    dve.sem_inc(free[st], 1)
                dve.sem_inc(ln_in, NCH)

            pairs_done = [0]

            def ffn(st):
                def hidden(it, q):
                    dve.wait_ge(full[st], it * 4 + (2 * q + 2))
                    dve.wait_ge(silu_done[q], it + (1 + pairs_done[0]))
                    dve.tensor_tensor(chunks(HT[:, q, :]), chunks(SL[:, :]), banks(1), ALU.mult).then_inc(ht_done[q], 1)
                    dve.wait_ge(ht_done[q], it + (1 + pairs_done[0]))
                    dve.sem_inc(set_free[st][1], 1)

                def low(it, q):
                    dve.wait_ge(hh_done[q], it + (1 + pairs_done[0]))
                    dve.tensor_tensor(HL[:, q, :], HT[:, q, :], HHf[:, q, :], ALU.subtract).then_inc(hl_done[q], 1)

                def sums(it, first_time, last=False):
                    order = [(m, c) for c in range(NCH) for m in range(KT)] if last else \
                        [(m, c) for m in range(KT) for c in range(NCH)]
                    if first_time:
                        dve.wait_ge(wn_y, KT * NCH * (2 * (pairs_done[0] // FG) + 1))
                    for e, (m, c) in enumerate(order):
                        if last and e in (KT + 2, 2 * KT + 2):
                            wide_centre(L, c - 1)
                        y = Y[:, m, c * CH:(c + 1) * CH]
                        acc = PS[:, 6 + e % 2, 0:CH]
                        dve.wait_ge(y_full[e % 2], it * 12 + (e // 2 - 12 + 1 + 12 * pairs_done[0]))
                        if first_time:
                            ins = dve.scalar_tensor_tensor(out=y, in0=y, scalar=ALPHA, in1=acc, op0=ALU.mult, op1=ALU.add)
                        else:
                            ins = dve.tensor_tensor(y, y, acc, ALU.add)
                        ins.then_inc(y_free[e % 2], 1)
                        if last and m == KT - 1:
                            for q in range(2):
                                dve.wait_ge(y_free[q], 1 + 12 * (FG - 1 + pairs_done[0]) + (KT // 2) * (c + 1))
                            dve.sem_inc(ln_in, 1)

                for q in range(2):
                    hidden(0, q)
                    low(0, q)

                def step(it, first_time):
                    hidden(it, 0)
                    sums(it, first_time)
                    low(it, 0)
                    hidden(it, 1)
                    low(it, 1)

                step(1, True)
                with dve.Fori(2, FG) as it:
                    dve.wait_ge(y_free[0], it * 12 + (1 - 12 + 12 * pairs_done[0]))
                    dve.wait_ge(y_free[1], it * 12 + (1 - 12 + 12 * pairs_done[0]))
                    step(it, False)
                for q in range(2):
                    dve.wait_ge(y_free[q], 1 + 12 * (FG - 1 + pairs_done[0]))
                L = 2 * (pairs_done[0] // FG) + 2
                sums(FG, False, last=True)
                pairs_done[0] += FG

            for q in range(2):
                dve.sem_inc(y_free[q], 1)
            dve.wait_ge(x_again, 16 * KT)
            residual("out", 1)
            wide_norm(1, 0)
            ffn("f0")
            wide_norm(2, 16, started=True)

            dve.memset(UP[:, :, 0:PH], 0.0).then_inc(up_zero, 1)
            dve.wait_ge(up_zero, 1)
            dve.wait_ge(hp_loaded, 16 * KT)
            dve.wait_ge(inv_loaded, 16)
            for e, m in enumerate(POOL_ORDER):
                group = m // 2
                dve.wait_ge(up_in, 5 * e + 5)
                src, w = UP[:, m, :], 1
                for s in range(group + 1):
                    dst = SUM[:, s % 2, :]
                    lo = 2 * w - 1
                    link(dve.tensor_tensor(dst[:, lo:], src[:, lo:], src[:, lo - w:PUW - w], ALU.add))
                    src, w = dst, 2 * w
                link(dve.tensor_tensor(src[:, PH:PH + 16], src[:, PH:PH + 16], INV[:, group, :], ALU.mult))
                for lo, hi in ((PH, PUP), (PUP + PH, PUW)):
                    dve.scalar_tensor_tensor(out=UP[:, m, lo:hi], in0=src[:, lo:hi], scalar=1.0 / w, in1=UP[:, m, lo:hi],
                                             op0=ALU.mult, op1=ALU.subtract).then_inc(d_done, 1)
                dve.wait_ge(d_done, 2 * e + 2)
            for e, m in enumerate(POOL_ORDER):
                dve.wait_ge(dh_done, 2 * e + 2)
                link(dve.tensor_tensor(XL[:, m, 0:NP_TOK], UP[:, m, PH:PUP], XHf[:, m, 0:NP_TOK], ALU.subtract))
                dve.tensor_tensor(XL[:, m, NP_TOK:T].rearrange("p (b s) -> p b s", b=SB),
                                  UP[:, m, PUP:].rearrange("p (b u) -> p b u", b=SB)[:, :, PH:],
                                  XHf[:, m, NP_TOK:T].rearrange("p (b s) -> p b s", b=SB), ALU.subtract).then_inc(dl_done, 1)
            for e, m in enumerate(POOL_ORDER):
                dve.wait_ge(zh_done, e + 1)
                dve.scalar_tensor_tensor(out=chunks(XL[:, m, :]), in0=banks(e % 2), scalar=PR[:, PR_SC + m:PR_SC + m + 1],
                                         in1=chunks(XHf[:, m, :]), op0=ALU.mult, op1=ALU.subtract).then_inc(zl_done, 1)
                dve.wait_ge(zl_done, e + 1)
                dve.sem_inc(free["grp"], 1)
            dve.wait_ge(wn_y, KT * NCH * 2)
            residual("outc", 3)
            wide_norm(3, 32)
            ffn("f1")
            wide_norm(4, 48, started=True, last=True)


def constants():
    import numpy as np
    f = np.float32
    c = {}
    eye = np.eye(P, dtype=f)
    c["consts"] = np.stack([eye, np.full((P, P), 1.0 / D, f), np.full((P, P), 1.0 / (CT * P), f)], 1)
    inv = (f(10000.0) ** (-np.arange(HD // 2, dtype=f) / f(HD // 2))).astype(f)

    def tables(pos):
        ang = (pos.astype(f)[None, :] * inv[:, None]).astype(f)
        cos, sin = np.cos(ang).astype(f), np.sin(ang).astype(f)
        return np.concatenate([cos] * 4, 0), np.concatenate([-sin, sin, -sin, sin], 0)

    pos = np.concatenate([np.arange(NP_TOK), np.tile(NP_TOK + np.arange(SS), SB), np.zeros(TP - T, int)])
    c["cosT"], c["sinT"] = tables(pos)
    q = np.arange(P)
    k = np.arange(P)
    caus = np.where(k[None] <= q[:, None], 0, -BIG).astype(f)
    kw = np.arange(640)
    wm = np.where((kw[None] > q[:, None]) & (kw[None] <= 512 + q[:, None]), 0, -BIG).astype(f)
    cma, sb = np.zeros((P, QT_N, NB), f), np.zeros((P, QT_N, 16), f)
    blk = np.arange(16)
    for i in range(QT_N):
        t = i * P + q
        cma[:, i] = np.where(np.arange(NB)[None] * 32 + 31 <= t[:, None], 0, -BIG)
        cur = (t // 64)[:, None]
        forced = (blk[None] == 0) | (blk[None] == cur) | (blk[None] == cur - 1)
        sb[:, i] = np.where(blk[None] * 64 <= t[:, None], np.where(forced, 1.0e4, 0.0), -1.0e4)
    c["att_c"] = np.concatenate([caus, wm, cma.reshape(P, -1), (cma == 0).astype(f).reshape(P, -1),
                                 sb.reshape(P, -1)], 1)
    pair, tok = q // 32, q % SS
    same = ((pair[:, None] == pair[None]) & (tok[:, None] == tok[None])).astype(f)
    j = np.arange(W_HIST + SS)
    swm = np.where((j[None] > tok[:, None]) & (j[None] <= W_HIST + tok[:, None]), 0, -BIG).astype(f)
    new = np.where(np.arange(SS)[None] <= tok[:, None], 0, -BIG).astype(f)
    ssb = np.zeros((P, 17), f)
    ssb[:, [0, 15, 16]] = 1.0e4
    cc, cs = tables(np.tile(np.arange(NB) * 32 + 31, 1 + SB))
    c["smp_c"] = np.concatenate([same, swm, new, ssb, cc, cs, np.zeros((P, 3), f)], 1)
    iv = np.ones((P, 4, 16), f)
    for g, w in enumerate((2, 4, 8, 16)):
        iv[:, g] = (f(w) / np.minimum(np.arange(16) + 1, w).astype(f))[None]
    c["invc"] = iv
    return {n: np.ascontiguousarray(a, dtype=f) for n, a in c.items()}


def layouts(i):
    import numpy as np
    a = {}
    xs = np.concatenate([i["x_prompt"].reshape(NP_TOK, D), i["x_sample"].reshape(SB * SS, D),
                         np.zeros((TP - T, D), np.float32)], 0)
    a["xT"] = xs.T.reshape(KT, P, TP)
    w_in = i["w_in_a"][0]
    cols = {}
    for r in range(R):
        cols[f"q{r}"] = np.concatenate([np.arange(HD) + (g * R + r) * HD for g in range(G)])
    for n, name in enumerate(("kc", "vc", "ks", "vs", "kw", "vw")):
        cols[name] = 512 + n * P + np.arange(P)
    for c in range(CT):
        cols[f"ga{c}"] = 512 + 768 + 24 + c * P + np.arange(P)
        cols[f"gb{c}"] = 512 + 768 + 24 + 512 + c * P + np.arange(P)
    cols["gl"] = 512 + 768 + np.arange(24)

    def out_tiles(w):
        kk, n = w.shape
        return w.reshape(kk // P, P, n // P, P).transpose(2, 1, 0, 3).reshape(n // P, P, kk)

    def in_tile(name):
        w = w_in[:, cols[name]]
        if w.shape[1] < P:
            w = np.concatenate([w, np.zeros((D, P - w.shape[1]), w.dtype)], 1)
        return out_tiles(w)[0]

    def ffn_tiles(l):
        w1, w3 = out_tiles(i["w1"][l]), out_tiles(i["w3"][l])
        w2 = i["w2"][l].reshape(FT, P, D)
        t = [w1[0], w3[0], w1[1], w3[1]]
        for g in range(1, FG):
            t += [w1[2 * g], w3[2 * g], w2[2 * g - 2], w2[2 * g - 1], w1[2 * g + 1], w3[2 * g + 1]]
        return t + [w2[FT - 2], w2[FT - 1]]

    wo = i["w_out_a"][0]
    rows = np.concatenate([cols[f"q{r}"] for r in range(R)] + [np.arange(512, 1024)])
    grp = i["w_grp_c"][0][[m // 2 for m in POOL_ORDER[::2]]].reshape(2, 2, 2, P, 2, P)
    grp = grp.transpose(0, 3, 1, 4, 2, 5).reshape(2, P, 1024)
    a["wst"] = np.stack([in_tile(n) for n in IN_ORDER] + list(out_tiles(wo[rows])) + ffn_tiles(0)
                        + list(out_tiles(i["w_in_c"][0])[POOL_ORDER]) + list(grp) + list(out_tiles(i["w_out_c"][0])) + ffn_tiles(1))

    def per_feature(v):
        return v.reshape(-1, P).T

    cw = i["conv_w"][0].reshape(CW, CT, P).transpose(2, 1, 0).reshape(P, CT * CW)
    pr = [cw] + [per_feature(i[n][0]) for n in ("conv_b", "conv_ln_g", "conv_ln_b", "scale_c")]
    for l in range(2):
        pr += [per_feature(i[n][l]) for n in ("ln1_g", "ln1_b", "ln2_g", "ln2_b")]
    a["params"] = np.concatenate(pr, 1)
    a["pe_t"] = np.stack([np.concatenate([i[n][0].T] * 2, 0) for n in ("pe_cmp_k", "pe_cmp_v")], 1)
    for name, n in (("cw_k", "w_cmp_k"), ("cw_v", "w_cmp_v")):
        w = np.zeros((P, NB, P), np.float32)
        w[:HD, :, :HD] = w[HD:, :, HD:] = i[n][0].transpose(1, 0, 2)
        a[name] = w
    a["hist_c"] = i["state_conv"][0].reshape(SB, CW - 1, CT, P).transpose(3, 2, 0, 1)
    a["hist_p"] = i["state_pool"][0].reshape(SB, PH, KT, P).transpose(3, 2, 0, 1)
    c = i["cache_kv"][0].reshape(NPOOL, P, 4, P)
    a["cache"] = np.concatenate([c[:, :, 0:3].transpose(0, 3, 2, 1), c[:, :, 3:4]], 2)
    sw = i["state_win"][0].reshape(SB, W_HIST, 2, P)
    a["swk"] = sw[:, :, 0].transpose(0, 2, 1)
    a["swv"] = sw[:, :, 1].reshape(SB, 4, P, P).transpose(0, 2, 1, 3)
    a["win_past"] = sw[:, SS:]
    a["ptab"] = i["page_table"].reshape(1, SB * PAGES)
    return {n: np.ascontiguousarray(v) for n, v in a.items()}


_INS = ["xT", "wst", "params", "consts", "att_c", "smp_c", "cosT", "sinT", "pe_t", "cw_k", "cw_v", "hist_c", "hist_p",
        "invc", "cache", "swk", "swv", "win_past", "ptab"]
_OUTS = [("yT", (P, KT, TP)), ("kvT", (6, P, TP)), ("win_old", (SB, W_HIST - SS, 2, P)), ("convT", (P, CT, 9, CW - 1)),
         ("poolT", (P, KT, 9, PH))]


def results(o):
    import numpy as np
    y = o["yT"].transpose(2, 1, 0).reshape(TP, D)
    kvT, conv, pool = o["kvT"], o["convT"], o["poolT"]
    kv = kvT[:4].transpose(2, 0, 1).reshape(TP, 4, G, HD)
    win = kvT[4:].transpose(2, 0, 1).reshape(TP, 2, G, HD)
    new = win[NP_TOK:T].reshape(1, SB, SS, 2, G, HD)
    old = o["win_old"].reshape(1, SB, W_HIST - SS, 2, G, HD)
    conv = conv.transpose(2, 3, 1, 0).reshape(9, CW - 1, CT * P)
    pool = pool.transpose(2, 3, 1, 0).reshape(9, PH, D)
    return (y[None, :NP_TOK], y[NP_TOK:T].reshape(SB, SS, D), kv[None, None, :NP_TOK],
            kv[NP_TOK:T].reshape(1, SB, SS, 4, G, HD), win[None, None, NP_TOK - W_HIST:NP_TOK],
            np.concatenate([old, new], 2), conv[None, :1], conv[None, 1:], pool[None, :1], pool[None, 1:])


def kernel(**inputs):
    import numpy as _np
    import concourse.bacc as _bacc
    from concourse.bass_utils import run_bass_kernel_spmd as _run

    arrays = layouts({k: _np.asarray(v) for k, v in inputs.items()})
    arrays.update(constants())
    nc = _bacc.Bacc("TRN2", target_bir_lowering=False, num_devices=1)
    args = [nc.dram_tensor(n, arrays[n].shape, mybir.dt.from_np(arrays[n].dtype), kind="ExternalInput").ap()
            for n in _INS]
    args += [nc.dram_tensor(n, shape, F32, kind="ExternalOutput").ap() for n, shape in _OUTS]
    build(nc, *args)
    r = _run(nc, [arrays], core_ids=[0])
    return tuple(_np.ascontiguousarray(x) for x in results(r.results[0]))
```
